# Optimizing a Trainium2 kernel written in Bass

```python
import math
import numpy as np
import jax
import jax.numpy as jnp
from jax import lax

D_MODEL = 1024
BATCH = 1
SEQ = 256
DEPTH = 2

CTX_LEN = 256
GRID_W = 64
ROPE_BASE = 10000.0
EPS = 1e-6

DA_HEADS = 4
DA_DIM = 64
DA_VDIM = 2 * DA_DIM
Q_BLOCK = 128
SW_HEADS = 8
SW_KV_HEADS = 2
SW_GROUP = SW_HEADS // SW_KV_HEADS
SW_DIM = 64
WINDOW = 128
RT_HEADS = 4
RT_KDIM = 64
RT_VDIM = 128
RT_CHUNK = 128
BRANCH_W = 512
N_BRANCH = 3
SPLIT_SIZES = (
    DA_HEADS * 2 * DA_DIM, DA_HEADS * 2 * DA_DIM, DA_HEADS * DA_VDIM,
    SW_HEADS * SW_DIM, SW_KV_HEADS * SW_DIM, SW_KV_HEADS * SW_DIM,
    RT_HEADS * RT_KDIM, RT_HEADS * RT_KDIM, RT_HEADS * RT_VDIM,
    RT_HEADS * RT_VDIM,
    N_BRANCH * D_MODEL,
)
D_IN = sum(SPLIT_SIZES)
N_EXPERTS = 16
N_GROUPS = 4
EXPERTS_PER_GROUP = N_EXPERTS // N_GROUPS
TOP_K = 2
D_EXPERT = 512

kernel_name = "hybrid_diffusion_trunk_diffattn_swa_retnet_groupmoe"

def rms_norm(x, g):
    xf = x.astype(jnp.float32)
    y = xf * lax.rsqrt(jnp.mean(xf * xf, axis=-1, keepdims=True) + EPS)
    return (y * g.astype(jnp.float32)).astype(x.dtype)

def group_norm_heads(o, g):
    of = o.astype(jnp.float32)
    mu = jnp.mean(of, axis=-1, keepdims=True)
    var = jnp.mean(jnp.square(of - mu), axis=-1, keepdims=True)
    y = ((of - mu) * lax.rsqrt(var + EPS)).reshape(o.shape[0], o.shape[1], -1)
    return (y * g.astype(jnp.float32)).astype(o.dtype)

def adaln(cond, w, b):
    m = jax.nn.silu(cond) @ w + b
    return jnp.split(m[..., None, :], 6, axis=-1)

def modulate(h, shift, scale):
    return h * (1 + scale) + shift

def axial_rope(n_tokens, dim):
    n_rows = n_tokens // GRID_W
    quarter = dim // 4
    inv = ROPE_BASE ** (-jnp.arange(quarter, dtype=jnp.float32) / quarter)
    rows = jnp.repeat(jnp.arange(n_rows, dtype=jnp.float32), GRID_W)
    cols = jnp.tile(jnp.arange(GRID_W, dtype=jnp.float32), n_rows)
    ang = jnp.concatenate([rows[:, None] * inv, cols[:, None] * inv], axis=-1)
    return jnp.cos(ang), jnp.sin(ang)

def apply_rope(x, cos, sin):
    half = x.shape[-1] // 2
    shape = (cos.shape[0],) + (1,) * (x.ndim - 3) + (half,)
    cos, sin = cos.reshape(shape), sin.reshape(shape)
    x1, x2 = x[..., :half], x[..., half:]
    return jnp.concatenate([x1 * cos - x2 * sin, x2 * cos + x1 * sin], axis=-1).astype(x.dtype)

def split_heads(p):
    b, n = p.shape[:2]
    idx = np.cumsum(SPLIT_SIZES)[:-1].tolist()
    aq, ak, av, bq, bk, bv, cq, ck, cv, cg, gates = jnp.split(p, idx, axis=-1)
    return (aq.reshape(b, n, DA_HEADS, 2, DA_DIM), ak.reshape(b, n, DA_HEADS, 2, DA_DIM),
            av.reshape(b, n, DA_HEADS, DA_VDIM),
            bq.reshape(b, n, SW_HEADS, SW_DIM), bk.reshape(b, n, SW_KV_HEADS, SW_DIM),
            bv.reshape(b, n, SW_KV_HEADS, SW_DIM),
            cq.reshape(b, n, RT_HEADS, RT_KDIM), ck.reshape(b, n, RT_HEADS, RT_KDIM),
            cv.reshape(b, n, RT_HEADS, RT_VDIM), cg, gates)

def diff_softmax(q, k, v, lam):
    s = jnp.einsum('bqhmd,bkhmd->bhmqk', q, k).astype(jnp.float32) * (DA_DIM ** -0.5)
    p = jax.nn.softmax(s, axis=-1)
    a = p[:, :, 0] - lam * p[:, :, 1]
    return jnp.einsum('bhqk,bkhe->bqhe', a.astype(v.dtype), v)

def diff_attention_latent(q, k, v, kc, vc, lam):
    b, n = q.shape[:2]
    k_all = jnp.concatenate([kc, k], axis=1)
    v_all = jnp.concatenate([vc, v], axis=1)
    qb = jnp.moveaxis(q.reshape(b, n // Q_BLOCK, Q_BLOCK, DA_HEADS, 2, DA_DIM), 1, 0)
    o = lax.map(lambda blk: diff_softmax(blk, k_all, v_all, lam), qb)
    return jnp.moveaxis(o, 0, 1).reshape(b, n, DA_HEADS, DA_VDIM)

def diff_out(o, g, lam_init):
    o = rms_norm(o, g) * (1 - lam_init)
    return o.reshape(o.shape[0], o.shape[1], -1)

def window_attention_latent(q, k, v, kc, vc, sink):
    b, n = q.shape[:2]
    nb = n // WINDOW
    scale = SW_DIM ** -0.5
    qb = q.reshape(b, nb, WINDOW, SW_KV_HEADS, SW_GROUP, SW_DIM)
    pad = ((0, 0), (WINDOW, WINDOW), (0, 0), (0, 0))
    kp = jnp.pad(k, pad).reshape(b, nb + 2, WINDOW, SW_KV_HEADS, SW_DIM)
    vp = jnp.pad(v, pad).reshape(b, nb + 2, WINDOW, SW_KV_HEADS, SW_DIM)
    kb = jnp.concatenate([kp[:, :-2], kp[:, 1:-1], kp[:, 2:]], axis=2)
    vb = jnp.concatenate([vp[:, :-2], vp[:, 1:-1], vp[:, 2:]], axis=2)
    s_win = jnp.einsum('bnqkgd,bnskd->bnkgqs', qb, kb).astype(jnp.float32) * scale
    qpos = jnp.arange(WINDOW)[:, None]
    spos = jnp.arange(3 * WINDOW)[None, :]
    abs_k = jnp.arange(nb)[:, None, None] * WINDOW - WINDOW + spos
    valid = (jnp.abs(spos - WINDOW - qpos) <= WINDOW)[None] & (abs_k >= 0) & (abs_k < n)
    s_win = jnp.where(valid[None, :, None, None], s_win, -jnp.inf)
    s_ctx = jnp.einsum('bnqkgd,bckd->bnkgqc', qb, kc).astype(jnp.float32) * scale
    s_sink = jnp.broadcast_to(sink.astype(jnp.float32).reshape(1, 1, SW_KV_HEADS, SW_GROUP, 1, 1),
                              s_win.shape[:-1] + (1,))
    p = jax.nn.softmax(jnp.concatenate([s_sink, s_ctx, s_win], axis=-1), axis=-1)
    n_ctx = kc.shape[1]
    p_ctx = p[..., 1:1 + n_ctx].astype(v.dtype)
    p_win = p[..., 1 + n_ctx:].astype(v.dtype)
    o = (jnp.einsum('bnkgqc,bckd->bnqkgd', p_ctx, vc)
         + jnp.einsum('bnkgqs,bnskd->bnqkgd', p_win, vb))
    return o.reshape(b, n, SW_HEADS * SW_DIM)

def window_attention_context(qc, kc, vc, sink):
    b, n = qc.shape[:2]
    qg = qc.reshape(b, n, SW_KV_HEADS, SW_GROUP, SW_DIM)
    s = jnp.einsum('bqkgd,bckd->bkgqc', qg, kc).astype(jnp.float32) * (SW_DIM ** -0.5)
    s_sink = jnp.broadcast_to(sink.astype(jnp.float32).reshape(1, SW_KV_HEADS, SW_GROUP, 1, 1),
                              s.shape[:-1] + (1,))
    p = jax.nn.softmax(jnp.concatenate([s_sink, s], axis=-1), axis=-1)[..., 1:]
    o = jnp.einsum('bkgqc,bckd->bqkgd', p.astype(vc.dtype), vc)
    return o.reshape(b, n, SW_HEADS * SW_DIM)

def retention_scan(q, k, v, log_gamma, state0):
    b, n = q.shape[:2]
    nc = n // RT_CHUNK
    lg = log_gamma.astype(jnp.float32)
    pos = jnp.arange(RT_CHUNK, dtype=jnp.float32)
    diff = pos[:, None] - pos[None, :]
    decay = jnp.where(diff >= 0, jnp.exp(jnp.maximum(diff, 0.0)[None] * lg[:, None, None]), 0.0)
    q_decay = jnp.exp((pos + 1)[:, None] * lg)[..., None]
    k_decay = jnp.exp((RT_CHUNK - 1 - pos)[:, None] * lg)[..., None]
    chunk_decay = jnp.exp(RT_CHUNK * lg)[:, None, None]

    def step(state, xs):
        qc, kc, vc = xs
        inner = jnp.einsum('bqhd,bkhd->bhqk', qc, kc) * decay
        o = (jnp.einsum('bhqk,bkhe->bqhe', inner, vc)
             + jnp.einsum('bqhd,bhde->bqhe', qc * q_decay, state))
        state = state * chunk_decay + jnp.einsum('bkhd,bkhe->bhde', kc * k_decay, vc)
        return state, o

    xs = tuple(jnp.swapaxes(t.astype(jnp.float32).reshape(b, nc, RT_CHUNK, RT_HEADS, -1), 0, 1)
               for t in (q, k * (RT_KDIM ** -0.5), v))
    state, o = lax.scan(step, state0, xs)
    return jnp.swapaxes(o, 0, 1).reshape(b, n, RT_HEADS, RT_VDIM).astype(v.dtype), state

def bi_retention(q, k, v, qc, kc, vc, log_gamma):
    zero = jnp.zeros((q.shape[0], RT_HEADS, RT_KDIM, RT_VDIM), jnp.float32)
    flip = lambda t: jnp.flip(t, axis=1)
    oc_f, st_f = retention_scan(qc, kc, vc, log_gamma[0], zero)
    oc_b, st_b = retention_scan(flip(qc), flip(kc), flip(vc), log_gamma[1], zero)
    ox_f, _ = retention_scan(q, k, v, log_gamma[0], st_f)
    ox_b, _ = retention_scan(flip(q), flip(k), flip(v), log_gamma[1], st_b)
    return ox_f + flip(ox_b), oc_f + flip(oc_b)

def retention_out(o, gate, gn_g):
    return group_norm_heads(o, gn_g) * jax.nn.silu(gate)

def merge_branches(oa, ob, oc, gate_logits, w_branch, w_out):
    ga, gb, gc = jnp.split(jax.nn.sigmoid(gate_logits), N_BRANCH, axis=-1)
    y = ga * (oa @ w_branch[0]) + gb * (ob @ w_branch[1]) + gc * (oc @ w_branch[2])
    return y @ w_out

def token_mixers(hx, hc, cos, sin, w_in, lam_vec, lam_init, subln_g, sink, ret_decay, ret_gn_g,
                 w_branch, w_out, ctx_out):
    aq, ak, av, bq, bk, bv, cq, ck, cv, cg, gates = split_heads(hx @ w_in)
    aqc, akc, avc, bqc, bkc, bvc, cqc, ckc, cvc, cgc, gates_c = split_heads(hc @ w_in)
    aq, ak, bq, bk = (apply_rope(t, cos, sin) for t in (aq, ak, bq, bk))
    lv = lam_vec.astype(jnp.float32)
    lam = jnp.exp(jnp.sum(lv[0] * lv[1])) - jnp.exp(jnp.sum(lv[2] * lv[3])) + lam_init
    log_gamma = jax.nn.log_sigmoid(ret_decay.astype(jnp.float32))
    ret_x, ret_c = bi_retention(cq, ck, cv, cqc, ckc, cvc, log_gamma)
    y_x = merge_branches(diff_out(diff_attention_latent(aq, ak, av, akc, avc, lam), subln_g, lam_init),
                         window_attention_latent(bq, bk, bv, bkc, bvc, sink),
                         retention_out(ret_x, cg, ret_gn_g), gates, w_branch, w_out)
    if not ctx_out:
        return y_x, None
    y_c = merge_branches(diff_out(diff_softmax(aqc, akc, avc, lam), subln_g, lam_init),
                         window_attention_context(bqc, bkc, bvc, sink),
                         retention_out(ret_c, cgc, ret_gn_g), gates_c, w_branch, w_out)
    return y_x, y_c

def grouped_moe(h, router_w, router_b, w_gate, w_up, w_down):
    scores = jax.nn.sigmoid((h @ router_w).astype(jnp.float32))
    biased = scores + router_b.astype(jnp.float32)
    grouped = biased.reshape(biased.shape[:-1] + (N_GROUPS, EXPERTS_PER_GROUP))
    group_score = lax.top_k(grouped, TOP_K)[0].sum(-1)
    best = jnp.argmax(group_score, axis=-1)
    in_group = (best[..., None] == jnp.arange(N_GROUPS))[..., None]
    masked = jnp.where(in_group, grouped, -jnp.inf).reshape(biased.shape)
    _, idx = lax.top_k(masked, TOP_K)
    w = jnp.take_along_axis(scores, idx, axis=-1)
    w = w / jnp.sum(w, axis=-1, keepdims=True)
    combine = jnp.einsum('bnk,bnke->bne', w, jax.nn.one_hot(idx, N_EXPERTS, dtype=jnp.float32)).astype(h.dtype)
    out = jnp.zeros_like(h)
    for e in range(N_EXPERTS):
        he = jax.nn.silu(h @ w_gate[e]) * (h @ w_up[e])
        out = out + combine[..., e:e + 1] * (he @ w_down[e])
    return out

def setup_inputs(seed: int = 0) -> dict:
    key = jax.random.key(seed)
    ks = jax.random.split(key, 24)
    nrm = lambda k, shape, s: jax.random.normal(k, shape, jnp.float32) * s
    L, D, E, F = DEPTH, D_MODEL, N_EXPERTS, D_EXPERT
    gamma_logit = jnp.log(2.0 ** (5.0 + jnp.arange(RT_HEADS, dtype=jnp.float32)) - 1.0)
    return {
        "x": nrm(ks[0], (BATCH, SEQ, D), 1.0),
        "c": nrm(ks[1], (BATCH, D), 1.0),
        "ctx": nrm(ks[2], (BATCH, CTX_LEN, D), 1.0),
        "c_ctx": nrm(ks[3], (D,), 1.0),
        "w_ada": nrm(ks[4], (L, D, 6 * D), 0.5 * D ** -0.5),
        "b_ada": nrm(ks[5], (L, 6 * D), 0.01),
        "norm_mix_g": 1.0 + nrm(ks[6], (L, D), 0.05),
        "norm_ffn_g": 1.0 + nrm(ks[7], (L, D), 0.05),
        "w_in": nrm(ks[8], (L, D, D_IN), D ** -0.5),
        "diff_lambda": nrm(ks[9], (L, 4, DA_DIM), 0.1),
        "diff_subln_g": 1.0 + nrm(ks[10], (L, DA_VDIM), 0.05),
        "swa_sink": nrm(ks[11], (L, SW_HEADS), 0.5),
        "ret_decay": gamma_logit + nrm(ks[12], (L, 2, RT_HEADS), 0.1),
        "ret_gn_g": 1.0 + nrm(ks[13], (L, RT_HEADS * RT_VDIM), 0.05),
        "w_branch": nrm(ks[14], (L, N_BRANCH, BRANCH_W, D), BRANCH_W ** -0.5),
        "w_out": nrm(ks[15], (L, D, D), D ** -0.5),
        "router_w": nrm(ks[16], (D, E), D ** -0.5),
        "router_b": nrm(ks[17], (E,), 0.01),
        "w_exp_gate": nrm(ks[18], (L, E, D, F), D ** -0.5),
        "w_exp_up": nrm(ks[19], (L, E, D, F), D ** -0.5),
        "w_exp_down": nrm(ks[20], (L, E, F, D), F ** -0.5),
        "final_g": 1.0 + nrm(ks[21], (D,), 0.05),
    }

def reference(x, c, ctx, c_ctx, w_ada, b_ada, norm_mix_g, norm_ffn_g, w_in, diff_lambda, diff_subln_g,
              swa_sink, ret_decay, ret_gn_g, w_branch, w_out, router_w, router_b, w_exp_gate, w_exp_up,
              w_exp_down, final_g):
    cos, sin = axial_rope(x.shape[1], DA_DIM)
    for l in range(DEPTH):
        ctx_out = l < DEPTH - 1
        lam_init = 0.8 - 0.6 * math.exp(-0.3 * l)
        sh1, sc1, g1, sh2, sc2, g2 = adaln(c, w_ada[l], b_ada[l])
        csh1, csc1, cg1, csh2, csc2, cg2 = adaln(c_ctx, w_ada[l], b_ada[l])
        hx = modulate(rms_norm(x, norm_mix_g[l]), sh1, sc1)
        hc = modulate(rms_norm(ctx, norm_mix_g[l]), csh1, csc1)
        y_x, y_c = token_mixers(hx, hc, cos, sin, w_in[l], diff_lambda[l], lam_init, diff_subln_g[l],
                                swa_sink[l], ret_decay[l], ret_gn_g[l], w_branch[l], w_out[l], ctx_out)
        x = x + g1 * y_x
        hx2 = modulate(rms_norm(x, norm_ffn_g[l]), sh2, sc2)
        x = x + g2 * grouped_moe(hx2, router_w, router_b, w_exp_gate[l], w_exp_up[l], w_exp_down[l])
        if ctx_out:
            ctx = ctx + cg1 * y_c
            hc2 = modulate(rms_norm(ctx, norm_ffn_g[l]), csh2, csc2)
            ctx = ctx + cg2 * grouped_moe(hc2, router_w, router_b, w_exp_gate[l], w_exp_up[l], w_exp_down[l])
    return rms_norm(x, final_g)


_drawn_inputs = setup_inputs


def setup_inputs(seed=0):
    import zlib

    import numpy as np

    out = dict(_drawn_inputs(seed))
    spreads = {}
    factors = {'swa_sink': 8.0}
    for name, (base, spread) in spreads.items():
        noise = np.random.default_rng([zlib.crc32(name.encode()), seed]).standard_normal(out[name].shape)
        drawn = base * np.exp(spread * noise) if base else spread * noise
        out[name] = jnp.asarray(drawn.astype(out[name].dtype))
    for name, factor in factors.items():
        out[name] = (out[name] * factor).astype(out[name].dtype)
    return out
```

```python
import math
from contextlib import ExitStack

import numpy as np

import concourse.bass as bass
from concourse import mybir

ALU = mybir.AluOpType
ACT = mybir.ActivationFunctionType
AX = mybir.AxisListType
F32 = mybir.dt.float32
BF16 = mybir.dt.bfloat16
I32 = mybir.dt.int32

P = 128
D = 1024
KD = D // P
SEQ = 256
CTX = 256
TOK = CTX + SEQ
NT = TOK // P
XT = CTX // P
DEPTH = 2
GRID_W = 64
EPS = 1e-6
HD = 64
SCALE = HD ** -0.5
DA_H, SW_H, SW_KV, RT_H = 4, 8, 2, 4
WINDOW = 128
BW = 512
KB = BW // P
EXPERTS = 16
GROUPS = 4
FE = 512
KF = FE // P
COLS = 512
RING = 3
TILE = KD * COLS
CAP = 128
ROUNDS = TOK // CAP
NEG = -1e30
MODS = 6 * KD

AQ, AK, AV, BQ, BK, BV, CQ, CK, CV, CG, GATES = (int(v) for v in np.cumsum(
    [0, 512, 512, 512, 512, 128, 128, 256, 256, 512, 512]))
W_IN_TILES = [(AQ, 512), (AK, 512), (AV, 512), (BQ, 512), (BK, 512), (CK, 256), (CV, 512), (CG, 512)]

C_ID, C_COS, C_SIN, C_PERM, C_TRI, C_ONE, C_MUP, C_MLO, C_E, C_PRI, C_END = (int(v) for v in np.cumsum(
    [0, P, SEQ, SEQ, P, P, P, P, P, EXPERTS, EXPERTS]))
TAB = 384


def shape_constants():
    q = HD // 4
    inv = np.float32(10000.0) ** (-np.arange(q, dtype=np.float32) / np.float32(q))
    t = np.arange(SEQ)
    rows, cols = (t // GRID_W).astype(np.float32), (t % GRID_W).astype(np.float32)
    ang = np.concatenate([rows[:, None] * inv, cols[:, None] * inv], axis=-1).astype(np.float32)
    d = np.arange(P) % HD
    cos, sin = np.cos(ang)[:, d % 32].T, np.sin(ang)[:, d % 32].T
    sin = np.where((d < 32)[:, None], -sin, sin)
    c = np.zeros((P, C_END), np.float32)
    i = np.arange(P)
    c[:, C_ID:C_ID + P] = np.eye(P)
    c[:, C_COS:C_COS + SEQ] = cos
    c[:, C_SIN:C_SIN + SEQ] = sin
    c[i ^ 32, C_PERM + i] = 1.0
    c[:, C_TRI:C_TRI + P] = i[:, None] < i[None, :]
    c[:, C_ONE:C_ONE + P] = 1.0
    c[:, C_MUP:C_MUP + P] = np.where(i[None, :] > i[:, None], NEG, 0.0)
    c[:, C_MLO:C_MLO + P] = np.where(i[None, :] < i[:, None], NEG, 0.0)
    c[:, C_E:C_E + EXPERTS] = np.arange(EXPERTS)
    c[:, C_PRI:C_PRI + EXPERTS] = EXPERTS - np.arange(EXPERTS)
    u0 = np.arange(TAB)[None, :] - P - i[:, None]
    u1 = np.arange(TAB)[None, :] + P
    r = np.zeros((P, 4, 2, TAB), np.float32)
    r[:, 0, 0], r[:, 0, 1] = np.maximum(u0, 0), u1 - i[:, None]
    r[:, 1, 0], r[:, 1, 1] = np.maximum(-u0, 0), 2 * CTX - u1 + i[:, None]
    r[:, 2, 0], r[:, 2, 1] = np.where(u0 >= 0, SCALE, 0.0), SCALE
    r[:, 3, 0], r[:, 3, 1] = np.where(u0 <= 0, SCALE, 0.0), SCALE
    return c, r.reshape(P, 8 * TAB)


def first_tile(l):
    return 0 if l < DEPTH - 1 else XT


def weight_tiles():
    order = [("ada", 0, j) for j in range(4)]
    place = {}
    for l in range(DEPTH):
        for j in range(len(W_IN_TILES)):
            order.append(("in", l, j))
            if l == 0:
                order.append(("ada", 0, 4 + j))
        for n, b in enumerate(BRANCH_ORDER):
            order.append(("branch", l, b))
            for half in range(2):
                order.append(("gate", l, 2 * b + half))
            if l == 0:
                order += [("ada", 1, 3 * n + j) for j in range(3)]
        order += [("out", l, 0), ("out", l, 1)]
        if l == 0:
            order += [("ada", 1, 9 + j) for j in range(3)]
        place[("experts", l)] = len(order)
        order += [("expert", l, j) for j in range(3 * EXPERTS)]
    for n, key in enumerate(order):
        place[key] = n
    return order, place


UP_BANK, HID_BANK = (1, 7), (4, 0)
BRANCH_ORDER = (1, 2, 0)


class Steps:

    def __init__(self, engine, sem):
        self.engine, self.sem, self.n = engine, sem, 0

    def __call__(self, instruction):
        self.n += 1
        instruction.then_inc(self.sem, 1)
        self.engine.wait_ge(self.sem, self.n)


class Moe:

    def __init__(self, sem, name):
        self.gate = sem(name + "_gate_ready")
        self.up = sem(name + "_up_ready")
        self.rowsT = sem(name + "_rows_turned")
        self.hidT = sem(name + "_hidden_turned")
        self.down = sem(name + "_down_ready")
        self.silu = sem(name + "_silu_ready")
        self.rowsT_act = sem(name + "_rows_kept_act")
        self.rowsT_dve = sem(name + "_rows_kept_dve")
        self.hid = sem(name + "_hidden_ready")
        self.hidT_kept = sem(name + "_hidden_kept")
        self.y_act = sem(name + "_y_kept_act")
        self.y_dve = sem(name + "_y_kept_dve")
        self.idx = sem(name + "_tokens_in")
        self.rows = sem(name + "_rows_in")
        self.y = sem(name + "_y_out")


def trunk(nc, x, c, ctx, c_ctx, w_ada, b_ada, norm_mix_g, norm_ffn_g, w_in, diff_lambda, diff_subln_g,
          swa_sink, ret_decay, ret_gn_g, w_branch, w_out, router_w, router_b, w_exp_gate, w_exp_up,
          w_exp_down, final_g, consts, ret_consts, out):
    order, place = weight_tiles()

    ada_v = w_ada.rearrange("l (k p) (j c) -> l j p k c", p=P, c=COLS)
    in_v = w_in.rearrange("l (k p) c -> l p k c", p=P)
    branch_v = w_branch.rearrange("l b (k p) c -> l b p k c", p=P)
    out_v = w_out.rearrange("l (k p) (h c) -> l h p k c", p=P, c=COLS)
    gate_v = w_exp_gate.rearrange("l e (k p) c -> l e p k c", p=P)
    up_v = w_exp_up.rearrange("l e (k p) c -> l e p k c", p=P)
    down_v = w_exp_down.rearrange("l e (k p) c -> l e p k c", p=P)
    list_d = nc.dram_tensor("slot_tokens", (TOK * EXPERTS, 1), I32, kind="Internal").ap()
    h_d = nc.dram_tensor("moe_rows", (TOK, D), F32, kind="Internal").ap()
    y_d = nc.dram_tensor("moe_results", (TOK * EXPERTS, D), F32, kind="Internal").ap()
    mod_d = nc.dram_tensor("mod_rows", (DEPTH, 2 * MODS, P), F32, kind="Internal").ap()
    list_v = list_d.rearrange("(q e) o -> e q o", e=EXPERTS)
    y_v = y_d.rearrange("(q e) d -> e q d", e=EXPERTS)

    with ExitStack() as stack:
        def sb(name, cols, dt=F32):
            return stack.enter_context(nc.sbuf_tensor(name, [P, cols], dt))

        def sem(name):
            return stack.enter_context(nc.semaphore(name))

        res = sb("residual", NT * D)[:, :].rearrange("p (t d) -> p t d", t=NT)
        hT = sb("hT", KD * TOK)[:, :].rearrange("p (k t) -> p k t", k=KD)
        ring = sb("ring", RING * TILE)
        cst = sb("cst", C_END)
        ret_tab = sb("ret_tab", RT_H * 2 * TAB)[:, :].rearrange("p (h j u) -> p h j u", h=RT_H, j=2)
        mods = sb("mods", DEPTH * 2 * MODS)[:, :].rearrange("p (l c m) -> p l c m", l=DEPTH, c=2)
        b_col = sb("b_col", DEPTH * MODS)
        NCOL = 2 * KD + 4 * KD + DEPTH + DEPTH * KB
        p_col = sb("p_col", NCOL)
        condT = sb("condT", KD * 2)[:, :].rearrange("p (k c) -> p k c", c=2)
        sink = sb("sink", DEPTH * SW_H)
        rbias = sb("rbias", EXPERTS)
        loggam = sb("loggam", DEPTH * 2 * RT_H)
        lgwork = sb("lgwork", 4 * DEPTH * 2 * RT_H)[:, :].rearrange("p (a n) -> p a n", a=4)
        rw = sb("rw", KD * EXPERTS)[:, :].rearrange("p (k e) -> p k e", e=EXPERTS)
        lam = sb("lam", 10)
        eps = sb("eps", 1)
        ss = sb("ss", NT)
        rstd = sb("rstd", NT)
        st = sb("st", 2 * 16)[:, :].rearrange("p (b n) -> p b n", b=2)
        ssh = sb("ssh", NT * 4)[:, :].rearrange("p (t h) -> p t h", t=NT)
        rsh = sb("rsh", NT * 4)[:, :].rearrange("p (t h) -> p t h", t=NT)
        mnh = sb("mnh", NT * 4)[:, :].rearrange("p (t h) -> p t h", t=NT)
        ssc = sb("ssc", NT * 4)[:, :].rearrange("p (t h) -> p t h", t=NT)
        rsc = sb("rsc", NT * 4)[:, :].rearrange("p (t h) -> p t h", t=NT)

        def small(name, inner):
            return sb(name, NT * inner)[:, :].rearrange("p (t e) -> p t e", t=NT)

        score, biased, masked = small("score", EXPERTS), small("biased", EXPERTS), small("masked", EXPERTS)
        first, second, assign = small("first", EXPERTS), small("second", EXPERTS), small("assign", EXPERTS)
        rt_a, rt_b, pairs = small("rt_a", EXPERTS), small("rt_b", EXPERTS), small("pairs", 6 * GROUPS)
        gsum, gsel, gtmp = small("gsum", GROUPS), small("gsel", GROUPS), small("gtmp", GROUPS)
        top, wsel, dest = small("top", 1), small("wsel", 2), small("dest", 2)
        dest_i = sb("dest_i", NT * 2, I32)
        tok_i = sb("tok_i", NT, I32)
        count_i = sb("count_i", 1, I32)
        idx_i = sb("idx_i", 1, I32)
        zero_i = sb("zero_i", TOK * EXPERTS // P, I32)

        ARENA = 25088
        arena = sb("arena", ARENA)

        def region(at, n):
            assert at + n <= ARENA
            return arena[:, at:at + n]

        def chunks(at, k, n=TOK):
            return region(at, k * n).rearrange("p (k t) -> p k t", k=k)

        aqT, akT, bqT, bkT = chunks(0, 4), chunks(2048, 4), chunks(6144, 4), chunks(8192, 2)
        av, bv = chunks(4096, NT, BW), chunks(9216, NT, P)
        cqT, ckT = chunks(9728, 2), chunks(10752, 2)
        cv, cg = chunks(11776, NT, BW), chunks(13824, NT, BW)
        prob = chunks(15872, 2, 1024)
        probT = region(17920, 1024)
        o_tok = [chunks(23040, NT, BW), chunks(18944, NT, BW), chunks(20992, NT, BW)]
        bk_raw = region(17920, TOK)
        rope_tmp = chunks(15872, 2, SEQ)
        oT = [aqT, bqT, chunks(11776, KB)]
        yT = chunks(2048, KD)
        sig = chunks(15872, 2, TOK)
        ytmp = chunks(16896, 2)
        xn = chunks(18944, NT, D)
        junk = region(14336, 512).bitcast(BF16)
        ret_c = region(15872, 8 * TAB).rearrange("p (a u) -> p a u", a=4)
        ret_t = chunks(23040, 2, 2 * TAB)
        lam_in = region(0, DEPTH * 4 * HD)
        lam_t = region(512, DEPTH * 2 * HD)
        rows_in = chunks(1024, 2, P)
        g_row = chunks(23040, 2, D)
        fg_row = region(18944, D)
        ffn_row = chunks(18944, 4, D)
        h_tok = chunks(6144, NT, D)
        junk2 = region(17920, 512).bitcast(BF16)
        rows_e, rowsT_e = region(0, D), chunks(1024, KD, P)
        y_e = region(2048, D)
        mix_tmp = region(16896, D)
        fin_tmp = region(17920, BW)
        y_tok = region(10240, 4 * D).rearrange("p (b c d) -> p b c d", b=2, c=2)
        silu_e, hid_e, hidT_e = region(14336, FE), region(14848, FE), chunks(15360, KF, P)
        mod_sb = sb('mod_sb', P)

        ident = cst[:, C_ID:C_ID + P]
        cosT, sinT = cst[:, C_COS:C_COS + SEQ], cst[:, C_SIN:C_SIN + SEQ]
        perm, tri, ones = cst[:, C_PERM:C_PERM + P], cst[:, C_TRI:C_TRI + P], cst[:, C_ONE:C_ONE + P]
        m_up, m_lo = cst[:, C_MUP:C_MUP + P], cst[:, C_MLO:C_MLO + P]
        e_num, pri = cst[:, C_E:C_E + EXPERTS], cst[:, C_PRI:C_PRI + EXPERTS]
        PARAMS = 12
        PC_MIX, PC_FFN = 2 * KD, 2 * KD + DEPTH * KD
        PC_SUB, PC_GN = 2 * KD + 2 * DEPTH * KD, 2 * KD + 2 * DEPTH * KD + DEPTH

        ps = stack.enter_context(nc.psum_tensor("ps", [P, 8, 512], F32))

        param_in, x_in, const_in, ret_in = sem("param_in"), sem("x_in"), sem("const_in"), sem("ret_in")
        slot_in = [sem(f"slot{s}_in") for s in range(RING)]
        ada_ready = sem("ada_ready")
        eps_set = sem("eps_set")
        cols_turned, cols_kept = sem("cols_turned"), sem("cols_kept")
        cond_ready, lam_ready = sem("cond_ready"), sem("lam_ready")
        lam_exp, gam_ready = sem("lam_exp"), sem("gam_ready")
        mods_a, mods_b = sem("mods_a_ready"), sem("mods_b_ready")
        mods_turned, mods_kept, mods_out = sem("mods_turned"), sem("mods_kept"), sem("mods_out")
        ret_pow, ret_done = sem("ret_pow"), sem("ret_done")
        sq_ready, std_ready, xn_ready = sem("sq_ready"), sem("std_ready"), sem("xn_ready")
        xn_turned, h_act, h_dve = sem("xn_turned"), sem("h_kept_act"), sem("h_kept_dve")
        proj_ready, proj_act, proj_dve = sem("proj_ready"), sem("proj_kept_act"), sem("proj_kept_dve")
        rot_ready, rope_done, bk_done = sem("rot_ready"), sem("rope_done"), sem("bk_done")
        s_ready, c_masked, b_probs, a_exps = sem("scores_ready"), sem("c_masked"), sem("b_probs"), sem("a_exps")
        b_max, a_max, a_comb = sem("b_max"), sem("a_max"), sem("a_combined")
        t_ready, pt_act, pt_dve = sem("probs_turned"), sem("probs_kept_act"), sem("probs_kept_dve")
        o_ready, o_kept = sem("o_ready"), sem("o_kept")
        fin_sq, fin_std, fin_done = sem("branch_squares"), sem("branch_roots"), sem("branch_normed")
        o_turned, oT_ready = sem("o_turned"), sem("oT_ready")
        gate_ready, br_ready, sig_ready, y_acc = sem("gate_ready"), sem("br_ready"), sem("sig_ready"), sem("y_acc")
        wo_ready, x_mixed = sem("wo_ready"), sem("x_mixed")
        g1_in, ffn_in, g2_in, fg_in = sem("g1_rows_in"), sem("ffn_rows_in"), sem("g2_rows_in"), sem("fg_row_in")
        h2_ready, h2_out, h2_turned = sem("h2_ready"), sem("h2_out"), sem("h2_turned")
        h2_act, h2_dve = sem("h2_kept_act"), sem("h2_kept_dve")
        logits, scored, assigned = sem("logits_ready"), sem("scores_of_experts"), sem("assigned")
        placed, dest_ready, count_ready = sem("places_ready"), sem("dest_ready"), sem("count_ready")
        ids_ready, zero_ready, zeroed, listed = sem("ids_ready"), sem("zero_ready"), sem("list_zeroed"), sem("listed")
        picked = [sem("picked0"), sem("picked1")]
        x_done, f_ready, out_done = sem("x_done"), sem("final_ready"), sem("out_done")
        y_scaled = sem("y_scaled")
        moe = Moe(sem, "moe")
        more = [Moe(sem, f"more{l}") for l in range(DEPTH)]
        more_w = [[sem(f"more{l}_slot{s}_in") for s in range(3)] for l in range(DEPTH)]
        more_go = [sem(f"more{l}_go") for l in range(DEPTH)]
        dve_step, pool_step = sem("dve_step"), sem("pool_step")

        nq = [NT - first_tile(l) for l in range(DEPTH)]
        rows_of = [1 if first_tile(l) else 2 for l in range(DEPTH)]

        def before(counts, l):
            return sum(counts[:l])

        def projections(l):
            lo = first_tile(l) * P
            q, k = slice(lo, TOK), slice(0, TOK)
            jobs = [(0, "T", P * i, P, aqT[:, i, :], q, "rope") for i in range(4)]
            jobs += [(1, "T", P * i, P, akT[:, i, :], k, "rope") for i in range(4)]
            jobs += [(2, "tok", 0, 512, av, t, "dve") for t in range(NT)]
            jobs += [(3, "T", P * i, P, bqT[:, i, :], q, "rope") for i in range(4)]
            jobs += [(4, "T", 0, P, bk_raw, k, "bk")]
            jobs += [(4, "tok", P, P, bv, t, "dve") for t in range(NT)]
            jobs += [(4, "T", 2 * P + P * i, P, cqT[:, i, :], q, "dve") for i in range(2)]
            jobs += [(5, "T", P * i, P, ckT[:, i, :], k, "dve") for i in range(2)]
            jobs += [(6, "tok", 0, 512, cv, t, "dve") for t in range(NT)]
            jobs += [(7, "tok", 0, 512, cg, t, "silu") for t in range(first_tile(l), NT)]
            return jobs

        jobs = [projections(l) for l in range(DEPTH)]
        n_act = [sum(j[6] != "dve" for j in js) for js in jobs]
        n_dve = [sum(j[6] == "dve" for j in js) for js in jobs]
        n_rope = [sum(j[6] in ("rope", "bk") for j in js) for js in jobs]

        n_jobs = [len(js) for js in jobs]

        def kept_by(l, i):
            dve = jobs[l][i][6] == "dve"
            own = sum((j[6] == "dve") == dve for j in jobs[l][:i + 1])
            return (proj_dve, before(n_dve, l) + own) if dve else (proj_act, before(n_act, l) + own)

        def attention_units(l):
            q0 = first_tile(l)
            units = [("c", h, s) for s in ((0, XT) if l < DEPTH - 1 else (XT,)) for h in range(RT_H)]
            units += [("b", h, t) for t in range(q0, NT) for h in range(SW_H // 2)]
            units += [("a", h, t) for t in range(q0, NT) for h in range(DA_H)]
            return units

        units = [attention_units(l) for l in range(DEPTH)]
        n_units = [len(u) for u in units]

        def of_kind(l, i, kind):
            return (sum(u[0] in kind for m in range(l) for u in units[m])
                    + sum(u[0] in kind for u in units[l][:i + 1]))

        def released(eng, l, i):
            kind = units[l][i][0]
            eng.wait_ge({"c": c_masked, "b": b_probs, "a": a_exps}[kind], of_kind(l, i, kind))

        def keys(unit):
            return CTX if unit[2] < XT else TOK

        def slot(n):
            return ring[:, (n % RING) * TILE:(n % RING + 1) * TILE]

        def kview(n, cols=COLS):
            return slot(n)[:, 0:KD * cols].rearrange("p (k c) -> p k c", k=KD)

        def wide(n):
            return slot(n).rearrange("p (k c) -> p k c", k=KB)

        def arrived(eng, n):
            return eng.wait_ge(slot_in[n % RING], 16 * (n // RING + 1))

        GB = 3 * KD
        NORM = 2 * KD

        def multiplied(n):
            kind, l, j = order[n]
            if kind == "ada":
                return ada_ready, MODS // 4 * l + j + 1
            if kind == "in":
                return proj_ready, before(n_jobs, l) + sum(job[0] <= j for job in jobs[l])
            if kind == "gate":
                return gate_ready, GB * l + KD * BRANCH_ORDER.index(j // 2) + 4 * (j % 2) + 4
            if kind == "branch":
                return br_ready, GB * l + KD * BRANCH_ORDER.index(j) + KD
            if kind == "out":
                return wo_ready, 2 * before(nq, l + 1) + j - 1
            k = EXPERTS * l + j // 3 + 1
            return ((moe.gate, k), (moe.up, 2 * k), (moe.down, 2 * k))[j % 3]

        def picks(l, n):
            return before(nq, l) // 2 + n // 2 + 1

        block = stack.enter_context(nc.Block())

        @block.sync
        def _(sp):
            def source(key):
                kind, l, j = key
                if kind == "ada":
                    return ada_v[l, j]
                if kind == "in":
                    at, n = W_IN_TILES[j]
                    return in_v[l, :, :, at:at + n]
                if kind == "gate":
                    return in_v[l, :, :, GATES + COLS * j:GATES + COLS * (j + 1)]
                if kind == "branch":
                    return branch_v[l, j]
                return out_v[l, j]

            def load(n):
                kind, _, j = order[n]
                if n >= RING:
                    sp.wait_ge(*multiplied(n - RING))
                dst = wide(n) if kind == "branch" else kview(n, W_IN_TILES[j][1] if kind == "in" else COLS)
                sp.dma_start(dst, source(order[n])).then_inc(slot_in[n % RING], 16)

            def expert_tile(l, e, j, s, arrival):
                src = (gate_v, up_v, down_v)[j][l, e]
                dst = ring[:, s * TILE:(s + 1) * TILE].rearrange("p (k c) -> p k c", k=KF if j == 2 else KD)
                sp.dma_start(dst, src).then_inc(arrival, 16)

            def mod_row(l, cond, m, dst, done):
                src = mod_d[l, cond * MODS + m * KD:cond * MODS + (m + 1) * KD, :].rearrange("k c -> (k c)")
                sp.dma_start(dst, src.partition_broadcast(P)).then_inc(done, 16)

            n = 0
            for l in range(DEPTH):
                t0 = first_tile(l)
                conds = (0, 1) if t0 == 0 else (1,)
                while order[n] != ("out", l, 0):
                    load(n)
                    n += 1
                sp.wait_ge(oT_ready, 12 * (l + 1))
                sp.wait_ge(mods_out, 16 * (l + 1))
                for cnd in conds:
                    mod_row(l, cnd, 2, g_row[:, cnd, :], g1_in)
                for cnd in conds:
                    mod_row(l, cnd, 4, ffn_row[:, cnd, :], ffn_in)
                    mod_row(l, cnd, 3, ffn_row[:, 2 + cnd, :], ffn_in)
                while n < place[("experts", l)]:
                    load(n)
                    n += 1
                for t in range(t0, NT):
                    sp.wait_ge(h2_ready, before(nq, l) + t - t0 + 1)
                    sp.dma_start(h_d[P * t:P * (t + 1), :], h_tok[:, t, :]).then_inc(h2_out, 16)
                sp.wait_ge(x_mixed, 2 * before(nq, l + 1))
                for cnd in conds:
                    mod_row(l, cnd, 5, g_row[:, cnd, :], g2_in)

                n0 = place[("experts", l)]
                ws = [(n0 + j) % RING for j in range(3)]
                for j in range(3):
                    sp.wait_ge(*multiplied(n0 + j - RING))
                    expert_tile(l, 0, j, ws[j], slot_in[ws[j]])
                if l + 1 < DEPTH:
                    sp.wait_ge(std_ready, 2 * l + 2)
                    sp.dma_start(ret_c, ret_consts.rearrange("p (a u) -> p a u", a=4)).then_inc(ret_in, 16)

                def y_store(e):
                    sp.wait_ge(moe.y_act, EXPERTS * l + e + 1)
                    sp.wait_ge(moe.y_dve, EXPERTS * l + e + 1)
                    sp.dma_start(y_v[e, 0:CAP, :], y_e[0:CAP, :]).then_inc(moe.y, 16)

                with sp.Fori(0, EXPERTS - 1) as e:
                    for j in range(3):
                        sp.wait_ge((moe.gate, moe.up, moe.down)[j], (e + (EXPERTS * l + 1)) * (1 if j == 0 else 2))
                        expert_tile(l, e + 1, j, ws[j], slot_in[ws[j]])
                    y_store(e)
                y_store(EXPERTS - 1)
                n = n0 + 3 * EXPERTS

                sp.wait_ge(count_ready, l + 1)
                largest = sp.value_load(count_i[0:1, 0:1], min_val=0, max_val=TOK)
                with sp.If(largest > CAP):
                    m = more[l]
                    with sp.Fori(0, EXPERTS) as e:
                        with sp.Fori(1, ROUNDS) as r:
                            k = e * (ROUNDS - 1) + r
                            sp.wait_ge(more_go[l], k)
                            for j in range(3):
                                expert_tile(l, e, j, j, more_w[l][j])
                            sp.wait_ge(m.y_act, k)
                            sp.wait_ge(m.y_dve, k)
                            sp.dma_start(y_d.rearrange("(r q e) d -> r e q d", e=EXPERTS, q=CAP)[r, e],
                                         y_e[0:CAP, :]).then_inc(m.y, 16)
                sp.nop()
            sp.wait_ge(x_mixed, 2 * before(nq, DEPTH))
            sp.wait_ge(h2_ready, before(nq, DEPTH))
            sp.dma_start(fg_row, final_g.partition_broadcast(P)).then_inc(fg_in, 16)
            for t in range(XT, NT):
                sp.wait_ge(f_ready, t - XT + 1)
                sp.dma_start(out[0, P * (t - XT):P * (t - XT + 1), :], h_tok[:, t, :]).then_inc(out_done, 16)
            sp.wait_ge(out_done, 16 * (NT - XT))

        @block.tensor
        def _(pe):
            def product(dst, pairs):
                last = None
                for i, (a, b) in enumerate(pairs):
                    last = pe.matmul(dst, a, b, start=(i == 0), stop=(i == len(pairs) - 1))
                return last

            def ada_tile(l, j):
                n = place[("ada", l, j)]
                arrived(pe, n)
                w = kview(n)
                for i in range(4):
                    m = 4 * j + i
                    last = product(ps[:, 7, 2 * m:2 * m + 2],
                                   [(w[:, k, P * i:P * (i + 1)], condT[:, k, :]) for k in range(KD)])
                last.then_inc(ada_ready, 1)

            def mods_turn(l):
                pe.wait_ge(mods_b, l + 1)
                pe.transpose(ps[0:2 * MODS, 6, 0:P], mods[:, l, :, :].rearrange("p c m -> p (c m)"), ident)\
                  .then_inc(mods_turned, 1)

            pe.wait_ge(const_in, 16)
            pe.wait_ge(param_in, 16 * PARAMS)
            pe.transpose(ps[:, 0, 0:DEPTH * MODS], rows_in[0:DEPTH * MODS, 0, :], ident[0:DEPTH * MODS, 0:DEPTH * MODS])\
              .then_inc(cols_turned, 1)
            pe.transpose(ps[:, 1, 0:NCOL], rows_in[0:NCOL, 1, :], ident[0:NCOL, 0:NCOL]).then_inc(cols_turned, 1)
            pe.wait_ge(cond_ready, 1)
            for j in range(4):
                ada_tile(0, j)

            for l in range(DEPTH):
                t0 = first_tile(l)
                lo = t0 * P

                for u in range(NORM):
                    cnd, k = divmod(u, KD)
                    if k == 0:
                        pe.wait_ge(xn_ready, NT * l + 2 * cnd + 2)
                    if u >= 4:
                        v = NORM * l + u - 4
                        pe.wait_ge(h_act if v % 2 else h_dve, v // 2 + 1)
                    for i in range(2):
                        last = pe.transpose(ps[:, u % 4, P * i:P * (i + 1)],
                                            xn[:, 2 * cnd + i, P * k:P * (k + 1)], ident)
                    last.then_inc(xn_turned, 1)
                pe.wait_ge(h_act, KD * (l + 1))
                pe.wait_ge(h_dve, KD * (l + 1))

                rope = before(n_rope, l)
                pending = None
                banks = 0
                for i, (wt, form, at, width, dst, tok, keep) in enumerate(jobs[l]):
                    n = place[("in", l, wt)]
                    arrived(pe, n)
                    w = kview(n, W_IN_TILES[wt][1])
                    if i >= 4:
                        pe.wait_ge(*kept_by(l, i - 4))
                    bank = ps[:, i % 4, :]
                    if form == "T":
                        last = product(bank[:, 0:tok.stop - tok.start],
                                       [(w[:, k, at:at + width], hT[:, k, tok]) for k in range(KD)])
                    else:
                        last = product(bank[:, 0:width],
                                       [(hT[:, k, P * tok:P * (tok + 1)], w[:, k, at:at + width]) for k in range(KD)])
                    last.then_inc(proj_ready, 1)
                    def rotate(i, raw):
                        pe.wait_ge(*kept_by(l, i))
                        if rope >= 2:
                            pe.wait_ge(rope_done, rope - 1)
                        pe.matmul(ps[:, 4 + rope % 2, 0:SEQ], perm, raw[:, CTX:TOK], start=True, stop=True)\
                          .then_inc(rot_ready, 1)
                    if pending is not None:
                        rotate(*pending)
                        rope += 1
                    pending = (i, dst) if keep in ("rope", "bk") else None
                    if i + 1 == len(jobs[l]) or jobs[l][i + 1][0] != wt:
                        if l == 0:
                            ada_tile(0, 4 + wt)
                if l == 0:
                    mods_turn(0)

                base = before(n_units, l)

                def scores(i):
                    kind, h, t = units[l][i]
                    g = base + i
                    if i >= 2:
                        released(pe, l, i - 2)
                    pair = ps[:, 2 * (g % 2):2 * (g % 2) + 2, :]
                    if kind == "c":
                        r = slice(HD * (h % 2), HD * (h % 2) + HD)
                        kts = range(0, XT) if t == 0 else range(0, NT)
                        q = cqT[r, h // 2, P * t:P * t + 2 * P]
                        for kt in kts:
                            last = pe.matmul(pair[:, kt // 2, 2 * P * (kt % 2):2 * P * (kt % 2 + 1)],
                                             ckT[r, h // 2, P * kt:P * (kt + 1)], q, start=True, stop=True)
                    elif kind == "b":
                        for j in range(2):
                            r = slice(HD * j, HD * (j + 1))
                            last = pe.matmul(pair[:, j, 0:keys(units[l][i])], bqT[r, h, P * t:P * (t + 1)],
                                             bkT[r, h // 2, 0:keys(units[l][i])], start=True, stop=True)
                    else:
                        for j in range(2):
                            r = slice(HD * j, HD * (j + 1))
                            last = pe.matmul(pair[:, j, 0:keys(units[l][i])], aqT[r, h, P * t:P * (t + 1)],
                                             akT[r, h, 0:keys(units[l][i])], start=True, stop=True)
                    last.then_inc(s_ready, 1)

                def turn(i):
                    kind, h, t = units[l][i]
                    if kind == "c":
                        return
                    g = base + i
                    done = of_kind(l, i, "ab")
                    if done >= 2:
                        pe.wait_ge(pt_act, done - 1)
                        pe.wait_ge(pt_dve, done - 1)
                    nk = keys(units[l][i]) // P
                    if kind == "b":
                        pe.wait_ge(b_probs, of_kind(l, i, "b"))
                        for j in range(2):
                            for k in range(nk):
                                last = pe.transpose(ps[:, 4 + j, P * k:P * (k + 1)],
                                                    prob[:, g % 2, 512 * j + P * k:512 * j + P * (k + 1)], ident)
                    else:
                        pe.wait_ge(a_comb, of_kind(l, i, "a"))
                        for k in range(nk):
                            hb, kb = divmod(k, nk // 2)
                            last = pe.transpose(ps[:, 4 + hb, P * kb:P * (kb + 1)],
                                                prob[:, g % 2, P * k:P * (k + 1)], ident)
                    last.then_inc(t_ready, 1)

                def outputs(i):
                    kind, h, t = units[l][i]
                    g = base + i
                    if g >= 2:
                        pe.wait_ge(o_kept, g - 1)
                    bank = ps[:, 6 + g % 2, :]
                    nk = keys(units[l][i]) // P
                    if kind == "c":
                        pe.wait_ge(c_masked, of_kind(l, i, "c"))
                        for q in range(2):
                            last = product(bank[:, P * q:P * (q + 1)],
                                           [(prob[:, g % 2, 256 * kt + P * q:256 * kt + P * (q + 1)],
                                             cv[:, kt, P * h:P * (h + 1)]) for kt in range(nk)])
                    else:
                        done = of_kind(l, i, "ab")
                        pe.wait_ge(pt_act, done)
                        pe.wait_ge(pt_dve, done)
                        if kind == "b":
                            for j in range(2):
                                kv = (2 * h + j) // (SW_H // SW_KV)
                                last = product(bank[:, HD * j:HD * (j + 1)],
                                               [(probT[:, 512 * j + P * k:512 * j + P * (k + 1)],
                                                 bv[:, k, HD * kv:HD * (kv + 1)]) for k in range(nk)])
                        else:
                            last = product(bank[:, 0:P],
                                           [(probT[:, P * k:P * (k + 1)], av[:, k, P * h:P * (h + 1)])
                                            for k in range(nk)])
                    last.then_inc(o_ready, 1)

                pe.wait_ge(proj_act, before(n_act, l + 1))
                pe.wait_ge(proj_dve, before(n_dve, l + 1))
                pe.wait_ge(rope_done, before(n_rope, l + 1))
                pe.wait_ge(bk_done, l + 1)
                if l == 0:
                    pe.wait_ge(mods_kept, 1)
                scores(0)
                scores(1)
                for i in range(n_units[l]):
                    turn(i)
                    if i + 2 < n_units[l]:
                        scores(i + 2)
                    outputs(i)

                released(pe, l, n_units[l] - 2)
                released(pe, l, n_units[l] - 1)
                pe.wait_ge(o_kept, base + n_units[l])
                for b_n, b in enumerate(BRANCH_ORDER):
                    if b != 1:
                        pe.wait_ge(fin_done, 2 * l + b_n)
                    for j in range(KB):
                        v = 12 * l + 4 * b_n + j
                        if v >= 2:
                            pe.wait_ge(oT_ready, v - 1)
                        for t in range(t0, NT):
                            last = pe.transpose(ps[:, 4 + j % 2, P * t:P * (t + 1)],
                                                o_tok[b][:, t, P * j:P * (j + 1)], ident)
                        last.then_inc(o_turned, 1)
                    wb = wide(place[("branch", l, b)])
                    for m in range(KD):
                        v = GB * l + KD * b_n + m
                        gate_n = place[("gate", l, 2 * b + m // 4)]
                        if m % 4 == 0:
                            arrived(pe, gate_n)
                        if v >= 2:
                            pe.wait_ge(sig_ready, v - 1)
                        wg = kview(gate_n)
                        last = product(ps[:, v % 2, lo:TOK],
                                       [(wg[:, k, P * (m % 4):P * (m % 4 + 1)], hT[:, k, lo:TOK]) for k in range(KD)])
                        last.then_inc(gate_ready, 1)
                        if m == 0:
                            arrived(pe, place[("branch", l, b)])
                            pe.wait_ge(oT_ready, 12 * l + 4 * b_n + 4)
                        if v >= 2:
                            pe.wait_ge(y_acc, v - 1)
                        last = product(ps[:, 2 + v % 2, lo:TOK],
                                       [(wb[:, k, P * m:P * (m + 1)], oT[b][:, k, lo:TOK]) for k in range(KB)])
                        last.then_inc(br_ready, 1)
                    if l == 0:
                        for j in range(3):
                            ada_tile(1, 3 * b_n + j)

                pe.wait_ge(y_acc, GB * (l + 1))
                n_out = place[("out", l, 0)]
                for t in range(t0, NT):
                    for half in range(2):
                        if t == t0:
                            arrived(pe, n_out + half)
                        v = 2 * before(nq, l) + 2 * (t - t0) + half
                        if v >= 2:
                            pe.wait_ge(x_mixed, v - 1)
                        w = kview(n_out + half)
                        last = product(ps[:, 4 + half, :],
                                       [(yT[:, k, P * t:P * (t + 1)], w[:, k, :]) for k in range(KD)])
                        last.then_inc(wo_ready, 1)
                if l == 0:
                    for j in range(9, 12):
                        ada_tile(1, j)

                for t in range(t0, NT):
                    pe.wait_ge(h2_ready, before(nq, l) + t - t0 + 1)
                    for half in range(2):
                        u = 2 * (t - t0) + half
                        if u >= 4:
                            v = 2 * before(nq, l) + u - 4
                            pe.wait_ge(h2_act if v % 2 else h2_dve, v // 2 + 1)
                        for k in range(4):
                            last = pe.transpose(ps[:, u % 4, P * k:P * (k + 1)],
                                                h_tok[:, t, P * (4 * half + k):P * (4 * half + k + 1)], ident)
                        last.then_inc(h2_turned, 1)
                pe.wait_ge(x_mixed, 2 * before(nq, l + 1))
                for t in range(t0, NT):
                    pe.wait_ge(h2_act, before(nq, l) + t - t0 + 1)
                    pe.wait_ge(h2_dve, before(nq, l) + t - t0 + 1)
                    last = product(ps[:, 4, EXPERTS * (t - t0):EXPERTS * (t - t0 + 1)],
                                   [(hT[:, k, P * t:P * (t + 1)], rw[:, k, :]) for k in range(KD)])
                last.then_inc(logits, 1)

                pe.wait_ge(assigned, l + 1)
                for t in range(nq[l]):
                    product(ps[:, 5, EXPERTS * t:EXPERTS * (t + 1)],
                            [(tri, assign[:, t, :])] + [(ones, assign[:, s, :]) for s in range(t)])
                product(ps[:, 5, 64:64 + EXPERTS], [(ones, assign[:, s, :]) for s in range(nq[l])])\
                    .then_inc(placed, 1)
                pe.wait_ge(count_ready, l + 1)
                if l == 0:
                    mods_turn(1)

                def turn_rows(m, k):
                    pe.wait_ge(m.rows, k * 16)
                    for j in range(KD):
                        last = pe.transpose(ps[:, 2 + j // 4, P * (j % 4):P * (j % 4) + CAP],
                                            rows_e[0:CAP, P * j:P * (j + 1)], ident[0:CAP, 0:CAP])
                    last.then_inc(m.rowsT, 1)

                def expert(m, k, ws, arrive, after):
                    pe.wait_ge(m.rowsT_act, k)
                    pe.wait_ge(m.rowsT_dve, k)
                    arrive(0)
                    wg, wu = (ring[:, s * TILE:(s + 1) * TILE].rearrange("p (k c) -> p k c", k=KD) for s in ws[:2])
                    wd = ring[:, ws[2] * TILE:(ws[2] + 1) * TILE].rearrange("p (k c) -> p k c", k=KF)
                    product(ps[0:CAP, 0, :], [(rowsT_e[:, j, 0:CAP], wg[:, j, :]) for j in range(KD)])\
                        .then_inc(m.gate, 1)
                    arrive(1)
                    for half in range(2):
                        c = slice(256 * half, 256 * (half + 1))
                        product(ps[0:CAP, UP_BANK[half], 0:256], [(rowsT_e[:, j, 0:CAP], wu[:, j, c]) for j in range(KD)])\
                            .then_inc(m.up, 1)
                    for half in range(2):
                        pe.wait_ge(m.hid, 2 * k - 1 + half)
                        for j in range(2 * half, 2 * half + 2):
                            last = pe.transpose(ps[:, HID_BANK[half], P * (j % 2):P * (j % 2) + CAP], hid_e[0:CAP, P * j:P * (j + 1)],
                                                ident[0:CAP, 0:CAP])
                        last.then_inc(m.hidT, 1)
                        if half == 0:
                            after()
                    arrive(2)
                    for part in range(2):
                        pe.wait_ge(m.hidT_kept, 2 * k - 1 + part)
                        for half in range(2):
                            for j in range(2 * part, 2 * part + 2):
                                last = pe.matmul(ps[0:CAP, 5 + half, :], hidT_e[:, j, 0:CAP],
                                                 wd[:, j, 512 * half:512 * (half + 1)],
                                                 start=(j == 0), stop=(j == KF - 1))
                            if part == 1:
                                last.then_inc(m.down, 1)

                n0 = place[("experts", l)]
                ws = [(n0 + j) % RING for j in range(3)]

                def main_expert(e, last):
                    k = e + (EXPERTS * l + 1)

                    def arrive(j):
                        pe.wait_ge(slot_in[ws[j]], e * 16 + 16 * ((n0 + j) // RING + 1))

                    expert(moe, k, ws, arrive, (lambda: None) if last else (lambda: turn_rows(moe, k + 1)))

                turn_rows(moe, EXPERTS * l + 1)
                with pe.Fori(0, EXPERTS - 1) as e:
                    main_expert(e, False)
                main_expert(EXPERTS - 1, True)

                largest = pe.value_load(count_i[0:1, 0:1], min_val=0, max_val=TOK)
                with pe.If(largest > CAP):
                    m = more[l]
                    pe.wait_ge(moe.y_act, EXPERTS * (l + 1))
                    pe.wait_ge(moe.y_dve, EXPERTS * (l + 1))
                    pe.nop().then_inc(more_go[l], 1)
                    with pe.Fori(0, EXPERTS) as e:
                        with pe.Fori(1, ROUNDS) as r:
                            k = e * (ROUNDS - 1) + r
                            turn_rows(m, k)
                            expert(m, k, (0, 1, 2), lambda j: pe.wait_ge(more_w[l][j], k * 16),
                                   lambda: None)
                            pe.wait_ge(m.down, k * 2)
                            pe.wait_ge(m.y_act, k)
                            pe.wait_ge(m.y_dve, k)
                            pe.nop().then_inc(more_go[l], 1)
                pe.nop()

        def keep_mods(act, l):
            act.wait_ge(mods_turned, l + 1)
            act.activation(mod_sb[0:2 * MODS, :], ps[0:2 * MODS, 6, 0:P], ACT.Copy).then_inc(mods_kept, 1)
            act.wait_ge(mods_kept, l + 1)
            act.dma_start(mod_d[l], mod_sb[0:2 * MODS, :]).then_inc(mods_out, 16)

        @block.scalar
        def _(act):
            act.dma_start(cst[:, :], consts).then_inc(const_in, 16)
            act.dma_start(rows_in[0:DEPTH * MODS, 0, :], b_ada.rearrange("l (m c) -> (l m) c", c=P)).then_inc(param_in, 16)
            at = 0
            for src in (c.rearrange("b (k c) -> (b k) c", c=P), c_ctx.rearrange("(k c) -> k c", c=P),
                        norm_mix_g.rearrange("l (k c) -> (l k) c", c=P), norm_ffn_g.rearrange("l (k c) -> (l k) c", c=P),
                        diff_subln_g, ret_gn_g.rearrange("l (k c) -> (l k) c", c=P)):
                act.dma_start(rows_in[at:at + src.shape[0], 1, :], src).then_inc(param_in, 16)
                at += src.shape[0]
            for dst, src in ((sink[:, :], swa_sink.rearrange("l h -> (l h)")), (rbias[:, :], router_b),
                             (loggam[:, :], ret_decay.rearrange("l f h -> (l f h)")),
                             (lam_in, diff_lambda.rearrange("l a d -> (l a d)"))):
                act.dma_start(dst, src.partition_broadcast(P)).then_inc(param_in, 16)
            act.dma_start(rw, router_w.rearrange("(k p) e -> p k e", p=P)).then_inc(param_in, 16)
            act.dma_start(res[:, 0:XT, :], ctx.rearrange("b (t p) d -> p (b t) d", p=P)).then_inc(x_in, 16)
            act.dma_start(res[:, XT:NT, :], x.rearrange("b (t p) d -> p (b t) d", p=P)).then_inc(x_in, 16)
            act.dma_start(ret_c, ret_consts.rearrange("p (a u) -> p a u", a=4)).then_inc(ret_in, 16)

            act.wait_ge(cols_turned, 2)
            act.activation(b_col[:, :], ps[:, 0, 0:DEPTH * MODS], ACT.Copy).then_inc(cols_kept, 1)
            for cnd, at in ((0, KD), (1, 0)):
                ins = act.activation(condT[:, :, cnd], ps[:, 1, at:at + KD], ACT.Silu)
                if cnd == 1:
                    ins.then_inc(cond_ready, 1)
            act.activation(p_col[:, :], ps[:, 1, 0:NCOL], ACT.Copy).then_inc(cols_kept, 1)
            act.wait_ge(lam_ready, 1)
            act.activation(lam[:, 4:8], lam[:, 0:4], ACT.Exp).then_inc(lam_exp, 1)
            act.activation(lgwork[:, 1, :], lgwork[:, 0, :], ACT.Exp).then_inc(lam_exp, 1)

            def squares(ready, junk_at, of, base):
                for n, t in enumerate(range(of, NT)):
                    ready(t, n)
                    if base - (NT - of) + n:
                        act.wait_ge(sq_ready, base - (NT - of) + n)
                    act.activation(junk_at, res[:, t, :], ACT.Square, accum_out=ss[:, t:t + 1]).then_inc(sq_ready, 1)
                act.wait_ge(sq_ready, base)
                act.activation(rstd[:, of:NT], ss[:, of:NT], ACT.Sqrt, bias=eps[:, :], scale=1.0 / D)\
                   .then_inc(std_ready, 1)

            act.wait_ge(x_in, 32)
            act.wait_ge(eps_set, 1)
            sq = 0
            for l in range(DEPTH):
                t0 = first_tile(l)

                def ready(t, n):
                    if l > 0:
                        act.wait_ge(x_done, before(nq, l - 1) + t + 1)
                sq += NT
                squares(ready, junk, 0, sq)

                act.wait_ge(ret_in, 16 * (l + 1))
                act.wait_ge(gam_ready, 1)
                for h in range(RT_H):
                    for f in range(2):
                        if h >= 1:
                            act.wait_ge(ret_done, RT_H * l + h)
                        g = (l * 2 + f) * RT_H + h
                        act.activation(ret_t[:, f, :], ret_c[:, f, :], ACT.Exp, scale=loggam[:, g:g + 1])\
                           .then_inc(ret_pow, 1)

                act.wait_ge(mods_a, l + 1)
                for u in range(1, NORM, 2):
                    cnd, k = divmod(u, KD)
                    act.wait_ge(xn_turned, NORM * l + u + 1)
                    act.activation(hT[:, k, 2 * P * cnd:2 * P * (cnd + 1)], ps[:, u % 4, 0:2 * P], ACT.Identity,
                                   bias=mods[:, l, cnd, k:k + 1], scale=mods[:, l, cnd, KD + k:KD + k + 1])\
                       .then_inc(h_act, 1)

                for i, (wt, form, at, width, dst, tok, keep) in enumerate(jobs[l]):
                    if keep == "dve":
                        continue
                    act.wait_ge(proj_ready, before(n_jobs, l) + i + 1)
                    if keep == "silu":
                        act.activation(dst[:, tok, :], ps[:, i % 4, :], ACT.Silu).then_inc(proj_act, 1)
                    else:
                        if keep == "bk":
                            act.wait_ge(ret_done, RT_H * (l + 1))
                        act.activation(dst[:, tok], ps[:, i % 4, 0:tok.stop - tok.start], ACT.Copy).then_inc(proj_act, 1)
                if l == 0:
                    keep_mods(act, 0)

                base = before(n_units, l)

                def exps(i):
                    kind, h, t = units[l][i]
                    if kind == "c":
                        return
                    g = base + i
                    nk = keys(units[l][i])
                    s = st[:, g % 2, :]
                    if i >= 2 and units[l][i - 2][0] == "c":
                        act.wait_ge(o_ready, g - 1)
                    act.wait_ge(b_max if kind == "b" else a_max, of_kind(l, i, kind))
                    for j in range(2):
                        ins = act.activation(prob[:, g % 2, 512 * j:512 * j + nk], ps[:, 2 * (g % 2) + j, 0:nk], ACT.Exp,
                                             bias=s[:, 2 + j:3 + j], scale=SCALE, accum_out=s[:, 4 + j:5 + j])
                    if kind == "b":
                        ins = act.activation(s[:, 8:10], s[:, 6:8], ACT.Exp)
                    ins.then_inc(b_probs if kind == "b" else a_exps, 1)

                def keep_turned(i):
                    kind, h, t = units[l][i]
                    if kind == "c":
                        return
                    nk = keys(units[l][i])
                    act.wait_ge(t_ready, of_kind(l, i, "ab"))
                    n = nk if kind == "b" else nk // 2
                    act.activation(probT[:, 0:n], ps[:, 4, 0:n], ACT.Copy).then_inc(pt_act, 1)

                exps(0)
                exps(1)
                for i in range(n_units[l]):
                    keep_turned(i)
                    if i + 2 < n_units[l]:
                        exps(i + 2)

                def roots():
                    act.wait_ge(fin_sq, 2 * (l + 1))
                    for a, r in ((ssc, rsc), (ssh, rsh)):
                        act.activation(r[:, t0:NT, :], a[:, t0:NT, :], ACT.Sqrt, bias=eps[:, :], scale=1.0 / P)\
                           .then_inc(fin_std, 1)

                for b_n, b in enumerate(BRANCH_ORDER):
                    if b_n == 0:
                        roots()
                    for j in range(KB):
                        act.wait_ge(o_turned, 12 * l + 4 * b_n + j + 1)
                        src = ps[:, 4 + j % 2, P * t0:TOK]
                        dst = oT[b][:, j, P * t0:TOK]
                        if b == 1:
                            ins = act.activation(dst, src, ACT.Copy)
                        elif b == 2:
                            ins = act.activation(dst, src, ACT.Copy, scale=p_col[:, PC_GN + KB * l + j:PC_GN + KB * l + j + 1])
                        else:
                            ins = act.activation(dst, src, ACT.Copy, scale=p_col[:, PC_SUB + l:PC_SUB + l + 1])
                        ins.then_inc(oT_ready, 1)
                    for m in range(KD):
                        v = GB * l + KD * b_n + m
                        act.wait_ge(gate_ready, v + 1)
                        if v >= 2:
                            act.wait_ge(y_acc, v - 1)
                        act.activation(sig[:, v % 2, P * t0:TOK], ps[:, v % 2, P * t0:TOK], ACT.Sigmoid)\
                           .then_inc(sig_ready, 1)

                def ready(t, n):
                    act.wait_ge(x_mixed, 2 * (before(nq, l) + n + 1))
                sq += nq[l]
                squares(ready, junk2, t0, sq)

                for u in range(1, 2 * nq[l], 2):
                    act.wait_ge(h2_turned, 2 * before(nq, l) + u + 1)
                    t = t0 + u // 2
                    act.activation(hT[:, 4:8, P * t:P * (t + 1)], ps[:, u % 4, :].rearrange("p (k t) -> p k t", k=4),
                                   ACT.Copy).then_inc(h2_act, 1)
                act.wait_ge(logits, l + 1)
                act.activation(score[:, 0:nq[l], :],
                               ps[:, 4, 0:EXPERTS * nq[l]].rearrange("p (t e) -> p t e", e=EXPERTS), ACT.Sigmoid)\
                   .then_inc(scored, 1)
                if l == 0:
                    keep_mods(act, 1)

                def keep_rows(m, k):
                    act.wait_ge(m.rowsT, k)
                    act.activation(rowsT_e[:, 0:4, 0:CAP], ps[:, 2, :].rearrange("p (k t) -> p k t", k=4)[:, :, 0:CAP],
                                   ACT.Copy).then_inc(m.rowsT_act, 1)

                def expert(m, k, next_rows, y_before):
                    act.wait_ge(m.gate, k)
                    act.activation(silu_e[0:CAP, :], ps[0:CAP, 0, :], ACT.Silu).then_inc(m.silu, 1)
                    if next_rows:
                        keep_rows(m, k + 1)
                    act.wait_ge(m.down, k * 2 - 1)
                    if y_before is not None:
                        act.wait_ge(m.y, y_before)
                    act.activation(y_e[0:CAP, 0:512], ps[0:CAP, 5, :], ACT.Copy).then_inc(m.y_act, 1)

                k0 = EXPERTS * l
                keep_rows(moe, k0 + 1)
                expert(moe, k0 + 1, True, 16 * k0 if k0 else None)
                with act.Fori(1, EXPERTS - 1) as e:
                    expert(moe, e + (k0 + 1), True, e * 16 + 16 * k0)
                expert(moe, k0 + EXPERTS, False, 16 * (k0 + EXPERTS - 1))
                largest = act.value_load(count_i[0:1, 0:1], min_val=0, max_val=TOK)
                with act.If(largest > CAP):
                    act.wait_ge(moe.y, 16 * EXPERTS * (l + 1))
                    with act.Fori(0, EXPERTS) as e:
                        with act.Fori(1, ROUNDS) as r:
                            k = e * (ROUNDS - 1) + r
                            keep_rows(more[l], k)
                            expert(more[l], k, False, None)
                            act.wait_ge(more[l].y, k * 16)
                for n in range(nq[l]):
                    act.wait_ge(picked[n % 2], 32 * picks(l, n))
                    act.activation(y_tok[:, n % 2, 0, :], y_tok[:, n % 2, 0, :], ACT.Copy, scale=wsel[:, n, 0:1])\
                       .then_inc(y_scaled, 1)

            def ready(t, n):
                act.wait_ge(x_done, before(nq, DEPTH - 1) + n + 1)
            sq += SEQ // P
            squares(ready, junk2, XT, sq)

        @block.vector
        def _(dve):
            step = Steps(dve, dve_step)

            def bc(ap, *shape):
                return ap.broadcast_to(shape)

            dve.memset(eps[:, :], EPS).then_inc(eps_set, 1)

            dve.wait_ge(param_in, 16 * PARAMS)
            lv = lam_in.rearrange("p (n a d) -> p n a d", a=2, d=HD)
            lt = lam_t.rearrange("p (n d) -> p n d", d=HD)
            step(dve.tensor_tensor(lt, lv[:, :, 0, :], lv[:, :, 1, :], ALU.mult))
            step(dve.tensor_reduce(lam[:, 0:4], lt, AX.X, ALU.add))
            dve.scalar_tensor_tensor(out=lgwork[:, 0, :], in0=loggam[:, :], scalar=-1.0, in1=loggam[:, :],
                                     op0=ALU.mult, op1=ALU.min).then_inc(lam_ready, 1)
            dve.wait_ge(lam_exp, 2)
            for l in range(DEPTH):
                init = 0.8 - 0.6 * math.exp(-0.3 * l)
                dve.scalar_tensor_tensor(out=lam[:, 8 + l:9 + l], in0=lam[:, 5 + 2 * l:6 + 2 * l], scalar=-init,
                                         in1=lam[:, 4 + 2 * l:5 + 2 * l], op0=ALU.add, op1=ALU.subtract)
            e_, s_, s2, acc = (lgwork[:, i, :] for i in (1, 2, 3, 0))
            step(dve.tensor_scalar(s_, e_, 2.0, None, ALU.add))
            step(dve.reciprocal(s_, s_))
            step(dve.tensor_tensor(s_, s_, e_, ALU.mult))
            step(dve.tensor_tensor(s2, s_, s_, ALU.mult))
            step(dve.tensor_scalar(acc, s2, 1.0 / 17, None, ALU.mult))
            for n in range(7, 0, -1):
                step(dve.scalar_tensor_tensor(out=acc, in0=acc, scalar=1.0 / (2 * n + 1), in1=s2,
                                              op0=ALU.add, op1=ALU.mult))
            step(dve.scalar_tensor_tensor(out=acc, in0=acc, scalar=1.0, in1=s_, op0=ALU.add, op1=ALU.mult))
            step(dve.tensor_scalar(acc, acc, 2.0, None, ALU.mult))
            dve.scalar_tensor_tensor(out=loggam[:, :], in0=loggam[:, :], scalar=0.0, in1=acc,
                                     op0=ALU.min, op1=ALU.subtract).then_inc(gam_ready, 1)
            dve.wait_ge(cols_kept, 2)
            for l in range(DEPTH):
                init = 0.8 - 0.6 * math.exp(-0.3 * l)
                step(dve.tensor_scalar(p_col[:, PC_SUB + l:PC_SUB + l + 1], p_col[:, PC_SUB + l:PC_SUB + l + 1],
                                       1.0 - init, None, ALU.mult))

            def modulation(l, lo, hi, scale_at, gain_at, done):
                m = mods[:, l, :, lo:hi]
                src = ps[:, 7, 0:2 * MODS].rearrange("p (m c) -> p c m", c=2)[:, :, lo:hi]
                b = b_col[:, MODS * l + lo:MODS * l + hi].unsqueeze(1)
                step(dve.tensor_tensor(m, src, bc(b, P, 2, hi - lo), ALU.add))
                m = mods[:, l, :, scale_at:scale_at + KD]
                g = p_col[:, gain_at + KD * l:gain_at + KD * (l + 1)].unsqueeze(1)
                dve.scalar_tensor_tensor(out=m, in0=m, scalar=1.0, in1=bc(g, P, 2, KD), op0=ALU.add, op1=ALU.mult)\
                   .then_inc(done, 1)

            roots = 0
            for l in range(DEPTH):
                t0 = first_tile(l)
                lo = P * t0

                dve.wait_ge(std_ready, 2 * l + 1)
                step(dve.reciprocal(rstd[:, :], rstd[:, :]))
                for t in range(NT):
                    dve.tensor_scalar(xn[:, t, :], res[:, t, :], rstd[:, t:t + 1], None, ALU.mult).then_inc(xn_ready, 1)

                for h in range(RT_H):
                    dve.wait_ge(ret_pow, 2 * (RT_H * l + h + 1))
                    for f in range(2):
                        step(dve.tensor_tensor(ret_t[:, f, :], ret_t[:, f, :], ret_c[:, 2 + f, :], ALU.mult))
                    dve.tensor_tensor(ret_tab[:, h, :, :].rearrange("p j u -> p (j u)"), ret_t[:, 0, :], ret_t[:, 1, :],
                                      ALU.add).then_inc(ret_done, 1)

                if l == 0:
                    dve.wait_ge(ada_ready, 4)
                    modulation(0, 0, 2 * KD, KD, PC_MIX, mods_a)
                dve.wait_ge(mods_a, l + 1)
                for u in range(0, NORM, 2):
                    cnd, k = divmod(u, KD)
                    dve.wait_ge(xn_turned, NORM * l + u + 1)
                    dve.tensor_scalar(hT[:, k, 2 * P * cnd:2 * P * (cnd + 1)], ps[:, u % 4, 0:2 * P],
                                      mods[:, l, cnd, KD + k:KD + k + 1], mods[:, l, cnd, k:k + 1], ALU.mult, ALU.add)\
                       .then_inc(h_dve, 1)

                def roped(dst, is_bk, n):
                    tmp, xs = rope_tmp[:, n % 2, :], dst[:, CTX:TOK]
                    dve.wait_ge(rot_ready, n + 1)
                    dve.tensor_tensor(tmp, ps[:, 4 + n % 2, 0:SEQ], sinT, ALU.mult)
                    step(dve.tensor_tensor(xs, xs, cosT, ALU.mult))
                    dve.tensor_tensor(xs, xs, tmp, ALU.add).then_inc(rope_done, 1)
                    if is_bk:
                        dve.wait_ge(rope_done, n + 1)
                        for kv in range(SW_KV):
                            for half in range(2):
                                ins = dve.tensor_copy(bkT[HD * half:HD * (half + 1), kv, :],
                                                      dst[HD * kv:HD * (kv + 1), :])
                                step(ins) if (kv, half) != (1, 1) else ins.then_inc(bk_done, 1)

                rope, pending = before(n_rope, l), None
                for i, (wt, form, at, width, dst, tok, keep) in enumerate(jobs[l]):
                    if keep == "dve":
                        dve.wait_ge(proj_ready, before(n_jobs, l) + i + 1)
                        out_ap = dst[:, tok] if form == "T" else dst[:, tok, 0:width]
                        n = width if form == "tok" else tok.stop - tok.start
                        dve.tensor_copy(out_ap, ps[:, i % 4, 0:n]).then_inc(proj_dve, 1)
                    if pending is not None:
                        roped(pending[0], pending[1], rope)
                        rope += 1
                    pending = (dst, keep == "bk") if keep in ("rope", "bk") else None
                if l == 0:
                    dve.wait_ge(ada_ready, MODS // 4)
                    modulation(0, 2 * KD, MODS, 4 * KD, PC_FFN, mods_b)

                base = before(n_units, l)

                def maxima(i):
                    kind, h, t = units[l][i]
                    g = base + i
                    s = st[:, g % 2, :]
                    pair = ps[:, 2 * (g % 2):2 * (g % 2) + 2, :]
                    dve.wait_ge(s_ready, g + 1)
                    nk = keys(units[l][i])
                    if kind == "c":
                        if i >= 2:
                            dve.wait_ge(o_ready, g - 1)
                        for kt in range(nk // P):
                            near = (t == 0) == (kt < XT)
                            at = P - P * (kt % XT)
                            ins = dve.tensor_tensor(prob[:, g % 2, 256 * kt:256 * (kt + 1)],
                                                    pair[:, kt // 2, 256 * (kt % 2):256 * (kt % 2 + 1)],
                                                    ret_tab[:, h, 0 if near else 1, at:at + 256], ALU.mult)
                        ins.then_inc(c_masked, 1)
                        return
                    if kind == "b" and t >= XT:
                        kt, mask = (NT - 1, m_up) if t == XT else (XT, m_lo)
                        part = pair[:, :, P * kt:P * (kt + 1)]
                        step(dve.tensor_tensor(part, part, bc(mask.unsqueeze(1), P, 2, P), ALU.add))
                    step(dve.tensor_reduce(s[:, 0:2], pair[:, :, 0:nk], AX.X, ALU.max))
                    if kind == "b":
                        sk = sink[:, SW_H * l + 2 * h:SW_H * l + 2 * h + 2]
                        step(dve.scalar_tensor_tensor(out=s[:, 0:2], in0=s[:, 0:2], scalar=SCALE, in1=sk,
                                                      op0=ALU.mult, op1=ALU.max))
                        dve.tensor_tensor(s[:, 6:8], sk, s[:, 0:2], ALU.subtract)
                        dve.tensor_scalar(s[:, 2:4], s[:, 0:2], -1.0, None, ALU.mult).then_inc(b_max, 1)
                    else:
                        dve.tensor_scalar(s[:, 2:4], s[:, 0:2], -SCALE, None, ALU.mult).then_inc(a_max, 1)

                def after_exps(i):
                    kind, h, t = units[l][i]
                    g = base + i
                    s = st[:, g % 2, :]
                    if g >= 2:
                        dve.wait_ge(o_kept, g - 1)
                    if kind == "b":
                        dve.wait_ge(b_probs, of_kind(l, i, "b"))
                        step(dve.tensor_tensor(s[:, 4:6], s[:, 4:6], s[:, 8:10], ALU.add))
                        step(dve.reciprocal(s[:, 10:12], s[:, 4:6]))
                    elif kind == "a":
                        nk = keys(units[l][i])
                        dve.wait_ge(a_exps, of_kind(l, i, "a"))
                        step(dve.reciprocal(s[:, 10:12], s[:, 4:6]))
                        step(dve.scalar_tensor_tensor(out=s[:, 12:13], in0=s[:, 4:5], scalar=s[:, 11:12],
                                                      in1=lam[:, 8 + l:9 + l], op0=ALU.mult, op1=ALU.mult))
                        dve.scalar_tensor_tensor(out=prob[:, g % 2, 0:nk], in0=prob[:, g % 2, 512:512 + nk],
                                                 scalar=s[:, 12:13], in1=prob[:, g % 2, 0:nk],
                                                 op0=ALU.mult, op1=ALU.add).then_inc(a_comb, 1)

                def keep_turned(i):
                    kind, h, t = units[l][i]
                    if kind == "c":
                        return
                    nk = keys(units[l][i])
                    dve.wait_ge(t_ready, of_kind(l, i, "ab"))
                    if kind == "b":
                        ins = dve.tensor_copy(probT[:, 512:512 + nk], ps[:, 5, 0:nk])
                    else:
                        ins = dve.tensor_copy(probT[:, nk // 2:nk], ps[:, 5, 0:nk // 2])
                    ins.then_inc(pt_dve, 1)

                def keep_output(i):
                    kind, h, t = units[l][i]
                    g = base + i
                    s = st[:, g % 2, :]
                    bank = ps[:, 6 + g % 2, :]
                    dve.wait_ge(o_ready, g + 1)
                    if kind == "c":
                        ins = dve.tensor_copy(o_tok[2][:, t:t + 2, P * h:P * (h + 1)],
                                              bank[:, 0:2 * P].rearrange("p (t e) -> p t e", t=2))
                    elif kind == "b":
                        ins = dve.tensor_tensor(o_tok[1][:, t, P * h:P * (h + 1)].rearrange("p (j e) -> p j e", j=2),
                                                bank[:, 0:P].rearrange("p (j e) -> p j e", j=2),
                                                bc(s[:, 10:12].unsqueeze(2), P, 2, HD), ALU.mult)
                    else:
                        ins = dve.tensor_scalar(o_tok[0][:, t, P * h:P * (h + 1)], bank[:, 0:P], s[:, 10:11], None,
                                                ALU.mult)
                    ins.then_inc(o_kept, 1)

                maxima(0)
                maxima(1)
                after_exps(0)
                for i in range(n_units[l]):
                    keep_turned(i)
                    if i + 1 < n_units[l]:
                        after_exps(i + 1)
                    if i + 2 < n_units[l]:
                        maxima(i + 2)
                    keep_output(i)

                dve.wait_ge(o_kept, base + n_units[l])
                heads = "p (h e) -> p h e"
                fin = fin_tmp.rearrange(heads, h=4)
                for t in range(t0, NT):
                    o = o_tok[2][:, t, :].rearrange(heads, h=4)
                    step(dve.tensor_reduce(mnh[:, t, :], o, AX.X, ALU.add))
                    step(dve.tensor_scalar(mnh[:, t, :], mnh[:, t, :], 1.0 / P, None, ALU.mult))
                    step(dve.tensor_tensor(o, o, bc(mnh[:, t, :].unsqueeze(2), P, 4, P), ALU.subtract))
                    step(dve.tensor_tensor(fin, o, o, ALU.mult))
                    ins = dve.tensor_reduce(ssc[:, t, :], fin, AX.X, ALU.add)
                    step(ins) if t < NT - 1 else ins.then_inc(fin_sq, 1)
                dve.wait_ge(fin_sq, 2 * l + 1)
                for t in range(t0, NT):
                    o = o_tok[0][:, t, :].rearrange(heads, h=4)
                    step(dve.tensor_tensor(fin, o, o, ALU.mult))
                    ins = dve.tensor_reduce(ssh[:, t, :], fin, AX.X, ALU.add)
                    step(ins) if t < NT - 1 else ins.then_inc(fin_sq, 1)

                def finish(b):
                    r = rsc if b == 2 else rsh
                    dve.wait_ge(fin_std, 2 * (l + 1))
                    step(dve.reciprocal(r[:, t0:NT, :], r[:, t0:NT, :]))
                    for t in range(t0, NT):
                        o = o_tok[b][:, t, :].rearrange(heads, h=4)
                        ins = dve.tensor_tensor(o, o, bc(r[:, t, :].unsqueeze(2), P, 4, P), ALU.mult)
                        if b == 2:
                            step(ins)
                            ins = dve.tensor_tensor(o_tok[2][:, t, :], o_tok[2][:, t, :], cg[:, t, :], ALU.mult)
                    ins.then_inc(fin_done, 1)

                for b_n, b in enumerate(BRANCH_ORDER):
                    for m in range(KD):
                        v = GB * l + KD * b_n + m
                        dve.wait_ge(br_ready, v + 1)
                        dve.wait_ge(sig_ready, v + 1)
                        y, sg, br = yT[:, m, lo:TOK], sig[:, v % 2, lo:TOK], ps[:, 2 + v % 2, lo:TOK]
                        if b_n == 0:
                            dve.tensor_tensor(y, sg, br, ALU.mult).then_inc(y_acc, 1)
                        else:
                            part = ytmp[:, v % 2, 0:TOK - lo]
                            dve.wait_ge(y_acc, v - 1)
                            step(dve.tensor_tensor(part, sg, br, ALU.mult))
                            dve.tensor_tensor(y, y, part, ALU.add).then_inc(y_acc, 1)
                        if b_n == 0 and m == 1:
                            finish(2)
                            finish(0)

                dve.wait_ge(g1_in, 16 * before(rows_of, l + 1))
                for t in range(t0, NT):
                    cnd = int(t >= XT)
                    for half in range(2):
                        v = 2 * before(nq, l) + 2 * (t - t0) + half
                        cols = slice(512 * half, 512 * (half + 1))
                        if v >= 2:
                            dve.wait_ge(x_mixed, v - 1)
                        dve.wait_ge(wo_ready, v + 1)
                        step(dve.tensor_tensor(mix_tmp[:, cols], ps[:, 4 + half, :], g_row[:, cnd, cols], ALU.mult))
                        dve.tensor_tensor(res[:, t, cols], res[:, t, cols], mix_tmp[:, cols], ALU.add)\
                           .then_inc(x_mixed, 1)

                dve.wait_ge(std_ready, 2 * l + 2)
                step(dve.reciprocal(rstd[:, t0:NT], rstd[:, t0:NT]))
                dve.wait_ge(ffn_in, 32 * before(rows_of, l + 1))
                for t in range(t0, NT):
                    cnd = int(t >= XT)
                    step(dve.scalar_tensor_tensor(out=h_tok[:, t, :], in0=res[:, t, :], scalar=rstd[:, t:t + 1],
                                                  in1=ffn_row[:, cnd, :], op0=ALU.mult, op1=ALU.mult))
                    dve.tensor_tensor(h_tok[:, t, :], h_tok[:, t, :], ffn_row[:, 2 + cnd, :], ALU.add)\
                       .then_inc(h2_ready, 1)
                for u in range(0, 2 * nq[l], 2):
                    dve.wait_ge(h2_turned, 2 * before(nq, l) + u + 1)
                    t = t0 + u // 2
                    dve.tensor_copy(hT[:, 0:4, P * t:P * (t + 1)], ps[:, u % 4, :].rearrange("p (k t) -> p k t", k=4))\
                       .then_inc(h2_dve, 1)

                n = nq[l]
                flat = lambda a: a[:, 0:n, :]
                grp = lambda a: a[:, 0:n, :].rearrange("p t (g e) -> p t g e", g=GROUPS)
                wide_e = (P, n, EXPERTS)
                dve.wait_ge(scored, l + 1)
                step(dve.tensor_tensor(flat(biased), flat(score), bc(rbias[:, :].unsqueeze(1), *wide_e), ALU.add))
                b4 = grp(biased)
                p6 = pairs[:, 0:n, :].rearrange("p t (g e) -> p t g e", g=GROUPS)
                at = 0
                for d in (1, 2, 3):
                    step(dve.tensor_tensor(p6[:, :, :, at:at + 4 - d], b4[:, :, :, 0:4 - d], b4[:, :, :, d:4], ALU.add))
                    at += 4 - d
                step(dve.tensor_reduce(flat(gsum), p6, AX.X, ALU.max))
                first_of(dve, step, bc, flat(gsum), flat(gsel), flat(gtmp), top[:, 0:n, :], pri[:, EXPERTS - GROUPS:EXPERTS], n, GROUPS)
                sel = bc(flat(gsel).unsqueeze(3), P, n, GROUPS, 4)
                step(dve.tensor_tensor(grp(masked), b4, sel, ALU.mult))
                step(dve.tensor_scalar(flat(gtmp), flat(gsel), -NEG, NEG, ALU.mult, ALU.add))
                step(dve.tensor_tensor(grp(masked), grp(masked), bc(flat(gtmp).unsqueeze(3), P, n, GROUPS, 4), ALU.add))
                first_of(dve, step, bc, flat(masked), flat(first), flat(rt_a), top[:, 0:n, :], pri, n, EXPERTS)
                step(dve.scalar_tensor_tensor(out=flat(masked), in0=flat(first), scalar=4 * NEG, in1=flat(masked),
                                              op0=ALU.mult, op1=ALU.add))
                first_of(dve, step, bc, flat(masked), flat(second), flat(rt_a), top[:, 0:n, :], pri, n, EXPERTS)
                dve.tensor_tensor(flat(assign), flat(first), flat(second), ALU.add).then_inc(assigned, 1)
                for j, chosen in ((0, first), (1, second)):
                    step(dve.tensor_tensor(flat(rt_a), flat(score), flat(chosen), ALU.mult))
                    step(dve.tensor_reduce(wsel[:, 0:n, j:j + 1], flat(rt_a), AX.X, ALU.add))
                step(dve.tensor_tensor(top[:, 0:n, :], wsel[:, 0:n, 0:1], wsel[:, 0:n, 1:2], ALU.add))
                step(dve.reciprocal(top[:, 0:n, :], top[:, 0:n, :]))
                step(dve.tensor_tensor(wsel[:, 0:n, :], wsel[:, 0:n, :], bc(top[:, 0:n, :], P, n, 2), ALU.mult))
                dve.wait_ge(placed, l + 1)
                step(dve.scalar_tensor_tensor(out=flat(rt_b), in0=ps[:, 5, 0:EXPERTS * n].rearrange(
                    "p (t e) -> p t e", e=EXPERTS), scalar=float(EXPERTS), in1=bc(e_num.unsqueeze(1), *wide_e),
                    op0=ALU.mult, op1=ALU.add))
                for j, chosen in ((0, first), (1, second)):
                    step(dve.tensor_tensor(flat(rt_a), flat(rt_b), flat(chosen), ALU.mult))
                    step(dve.tensor_reduce(dest[:, 0:n, j:j + 1], flat(rt_a), AX.X, ALU.add))
                dve.tensor_copy(dest_i[:, 0:2 * n], dest[:, 0:n, :].rearrange("p t j -> p (t j)")).then_inc(dest_ready, 1)
                step(dve.tensor_reduce(top[:, 0, 0:1], ps[:, 5, 64:64 + EXPERTS], AX.X, ALU.max))
                dve.tensor_copy(count_i[:, :], top[:, 0, 0:1]).then_inc(count_ready, 1)
                if l + 1 < DEPTH:
                    dve.wait_ge(ada_ready, MODS // 4 * (l + 2))
                    modulation(l + 1, 0, 2 * KD, KD, PC_MIX, mods_a)
                    modulation(l + 1, 2 * KD, MODS, 4 * KD, PC_FFN, mods_b)

                def keep_rows(m, k):
                    dve.wait_ge(m.rowsT, k)
                    dve.tensor_copy(rowsT_e[:, 4:8, 0:CAP], ps[:, 3, :].rearrange("p (k t) -> p k t", k=4)[:, :, 0:CAP])\
                       .then_inc(m.rowsT_dve, 1)

                def expert(m, k, next_rows, y_before):
                    dve.wait_ge(m.silu, k)
                    for half in range(2):
                        c = slice(256 * half, 256 * (half + 1))
                        dve.wait_ge(m.up, k * 2 - 1 + half)
                        dve.tensor_tensor(hid_e[0:CAP, c], silu_e[0:CAP, c], ps[0:CAP, UP_BANK[half], 0:256], ALU.mult)\
                           .then_inc(m.hid, 1)
                    for half in range(2):
                        dve.wait_ge(m.hidT, k * 2 - 1 + half)
                        dve.tensor_copy(hidT_e[:, 2 * half:2 * half + 2, 0:CAP],
                                        ps[:, HID_BANK[half], 0:256].rearrange("p (k t) -> p k t", k=2)[:, :, 0:CAP])\
                           .then_inc(m.hidT_kept, 1)
                    if next_rows:
                        keep_rows(m, k + 1)
                    dve.wait_ge(m.down, k * 2)
                    if y_before is not None:
                        dve.wait_ge(m.y, y_before)
                    dve.tensor_copy(y_e[0:CAP, 512:1024], ps[0:CAP, 6, :]).then_inc(m.y_dve, 1)

                k0 = EXPERTS * l
                keep_rows(moe, k0 + 1)
                expert(moe, k0 + 1, True, 16 * k0 if k0 else None)
                with dve.Fori(1, EXPERTS - 1) as e:
                    expert(moe, e + (k0 + 1), True, e * 16 + 16 * k0)
                expert(moe, k0 + EXPERTS, False, 16 * (k0 + EXPERTS - 1))
                largest = dve.value_load(count_i[0:1, 0:1], min_val=0, max_val=TOK)
                with dve.If(largest > CAP):
                    dve.wait_ge(moe.y, 16 * EXPERTS * (l + 1))
                    with dve.Fori(0, EXPERTS) as e:
                        with dve.Fori(1, ROUNDS) as r:
                            k = e * (ROUNDS - 1) + r
                            keep_rows(more[l], k)
                            expert(more[l], k, False, None)
                            dve.wait_ge(more[l].y, k * 16)

                dve.wait_ge(g2_in, 16 * before(rows_of, l + 1))
                for i in range(n):
                    t, cnd = t0 + i, int(t0 + i >= XT)
                    dve.wait_ge(picked[i % 2], 32 * picks(l, i))
                    dve.wait_ge(y_scaled, before(nq, l) + i + 1)
                    y1, y2 = y_tok[:, i % 2, 0, :], y_tok[:, i % 2, 1, :]
                    step(dve.scalar_tensor_tensor(out=y2, in0=y2, scalar=wsel[:, i, 1:2], in1=y1,
                                                  op0=ALU.mult, op1=ALU.add))
                    step(dve.tensor_tensor(y2, y2, g_row[:, cnd, :], ALU.mult))
                    dve.tensor_tensor(res[:, t, :], res[:, t, :], y2, ALU.add).then_inc(x_done, 1)

            dve.wait_ge(std_ready, 2 * DEPTH + 1)
            step(dve.reciprocal(rstd[:, XT:NT], rstd[:, XT:NT]))
            dve.wait_ge(fg_in, 16)
            for t in range(XT, NT):
                dve.scalar_tensor_tensor(out=h_tok[:, t, :], in0=res[:, t, :], scalar=rstd[:, t:t + 1],
                                         in1=fg_row, op0=ALU.mult, op1=ALU.mult).then_inc(f_ready, 1)

        @block.gpsimd
        def _(pool):
            pool.memset(zero_i[:, :], 0).then_inc(zero_ready, 1)
            pool.iota(tok_i[:, :], pattern=[[P, NT]], base=0, channel_multiplier=1).then_inc(ids_ready, 1)
            pool.wait_ge(zero_ready, 1)
            pool.dma_start(list_d.rearrange("(p n) o -> p (n o)", p=P), zero_i[:, :]).then_inc(zeroed, 16)
            pool.wait_ge(ids_ready, 1)
            pool.wait_ge(zeroed, 16)

            def gather(m, k, rows):
                pool.dma_start(idx_i[0:CAP, :], rows, allow_slow_non_contiguous=True).then_inc(m.idx, 16)
                pool.wait_ge(m.idx, k * 16)
                pool.sem_inc(pool_step, 1)
                pool.indirect_dma_start(out=rows_e[0:CAP, :], out_offset=None, in_=h_d,
                                        in_offset=bass.IndirectOffsetOnAxis(ap=idx_i[0:CAP, 0:1], axis=0))\
                    .then_inc(m.rows, 16)

            def pick(l, results):
                for i in range(nq[l]):
                    if i >= 2:
                        pool.wait_ge(x_done, before(nq, l) + i - 1)
                    for j in range(2):
                        pool.indirect_dma_start(out=y_tok[:, i % 2, j, :], out_offset=None, in_=results,
                                                in_offset=bass.IndirectOffsetOnAxis(
                                                    ap=dest_i[:, 2 * i + j:2 * i + j + 1], axis=0))\
                            .then_inc(picked[i % 2], 16)

            for l in range(DEPTH):
                t0 = first_tile(l)
                pool.wait_ge(dest_ready, l + 1)
                for t in range(nq[l]):
                    for j in range(2):
                        pool.indirect_dma_start(out=list_d, in_=tok_i[:, t0 + t:t0 + t + 1], in_offset=None,
                                                out_offset=bass.IndirectOffsetOnAxis(
                                                    ap=dest_i[:, 2 * t + j:2 * t + j + 1], axis=0)).then_inc(listed, 16)
                pool.wait_ge(listed, 32 * before(nq, l + 1))
                pool.wait_ge(h2_out, 16 * before(nq, l + 1))
                k0 = EXPERTS * l
                gather(moe, k0 + 1, list_v[0, 0:CAP, :])
                with pool.Fori(1, EXPERTS) as e:
                    pool.wait_ge(moe.rowsT, e + k0)
                    gather(moe, e + (k0 + 1), list_v[e, 0:CAP, :])
                pool.wait_ge(moe.y, 16 * EXPERTS * (l + 1))
                largest = pool.value_load(count_i[0:1, 0:1], min_val=0, max_val=TOK)
                with pool.If(largest > CAP):
                    with pool.Fori(0, EXPERTS) as e:
                        with pool.Fori(1, ROUNDS) as r:
                            k = e * (ROUNDS - 1) + r
                            pool.wait_ge(more_go[l], k)
                            gather(more[l], k, list_d.rearrange("(r q e) o -> r e q o", e=EXPERTS, q=CAP)[r, e])
                            pool.wait_ge(more[l].y, k * 16)
                    pick(l, y_d)
                with pool.Else():
                    pick(l, y_d[0:CAP * EXPERTS, :])
                pool.nop()


def first_of(dve, step, bc, values, chosen, tmp, top, priority, n, width):
    shape = (P, n, width)
    step(dve.tensor_reduce(top, values, AX.X, ALU.max))
    step(dve.tensor_tensor(tmp, values, bc(top, *shape), ALU.is_equal))
    step(dve.tensor_tensor(tmp, tmp, bc(priority.unsqueeze(1), *shape), ALU.mult))
    step(dve.tensor_reduce(top, tmp, AX.X, ALU.max))
    step(dve.tensor_tensor(chosen, tmp, bc(top, *shape), ALU.is_equal))


_INS = ['x', 'c', 'ctx', 'c_ctx', 'w_ada', 'b_ada', 'norm_mix_g', 'norm_ffn_g', 'w_in', 'diff_lambda', 'diff_subln_g',
        'swa_sink', 'ret_decay', 'ret_gn_g', 'w_branch', 'w_out', 'router_w', 'router_b', 'w_exp_gate', 'w_exp_up',
        'w_exp_down', 'final_g']


def kernel(**inputs):
    import numpy as _np
    import concourse.bacc as _bacc
    from concourse import mybir as _mybir
    from concourse.bass_utils import run_bass_kernel_spmd as _run

    nc = _bacc.Bacc("TRN2", target_bir_lowering=False, num_devices=1)
    arrays, args = {}, []
    values = [(name, _np.ascontiguousarray(inputs[name])) for name in _INS]
    values += list(zip(("consts", "ret_consts"), shape_constants()))
    for name, a in values:
        arrays[f"in_{name}"] = a
        args.append(nc.dram_tensor(f"in_{name}", a.shape, _mybir.dt.from_np(a.dtype), kind="ExternalInput").ap())
    out = nc.dram_tensor("out_0", (1, SEQ, D), F32, kind="ExternalOutput").ap()
    trunk(nc, *args, out)
    r = _run(nc, [arrays], core_ids=[0])
    return r.results[0]["out_0"]
```
